# Optimizing a Trainium2 kernel written in Bass

```python
import jax, jax.numpy as jnp
from jax import lax
import numpy as np

D_MODEL = 1024
BATCH = 1
SEQ = 1024
DEPTH = 1

CHUNK = 64
N_META = 16
BLOCK = 128
HEAD_DIM = 64
SWA_WINDOW = 128
SWA_WIN_CHUNKS = SWA_WINDOW // CHUNK
SWA_Q_HEADS = 8
SWA_KV_HEADS = 2
SWA_GROUP = SWA_Q_HEADS // SWA_KV_HEADS
SWA_WIDTH = SWA_Q_HEADS * HEAD_DIM
SWA_KV_WIDTH = SWA_KV_HEADS * HEAD_DIM
FOX_HEADS = 8
FOX_WIDTH = FOX_HEADS * HEAD_DIM
RMS_EPS = 1e-6
ATTN_SCALE = HEAD_DIM ** -0.5
NEG_INF = -1e30
IN_SPLITS = (SWA_WIDTH, SWA_KV_WIDTH, SWA_KV_WIDTH, SWA_WIDTH,
             FOX_WIDTH, FOX_WIDTH, FOX_WIDTH, FOX_WIDTH, FOX_HEADS,
             D_MODEL, D_MODEL)
D_IN = sum(IN_SPLITS)

kernel_name = "hybrid_swa_sink_fox_gated_block"

def _rmsnorm(x, g):
    x32 = x.astype(jnp.float32)
    y = x32 * lax.rsqrt(jnp.mean(x32 * x32, axis=-1, keepdims=True) + RMS_EPS)
    return (y * g.astype(jnp.float32)).astype(x.dtype)

def _alibi_slopes(n):
    return jnp.exp2(-8.0 * jnp.arange(1, n + 1, dtype=jnp.float32) / n)

def _attend_with_sinks(q, k, v, bias, sinks):
    logits = jnp.einsum('bntkgd,bnckd->bnkgtc', q, k).astype(jnp.float32) * ATTN_SCALE + bias
    sink = jnp.broadcast_to(sinks.astype(jnp.float32)[:, :, None, None], logits.shape[:-1] + (1,))
    probs = jax.nn.softmax(jnp.concatenate([logits, sink], axis=-1), axis=-1)[..., :-1]
    return jnp.einsum('bnkgtc,bnckd->bntkgd', probs.astype(v.dtype), v)

def _swa_branch(q, k, v, sinks):
    b, l = q.shape[0], q.shape[1]
    s = l - N_META
    nb = s // BLOCK
    slopes = _alibi_slopes(SWA_Q_HEADS).reshape(SWA_KV_HEADS, SWA_GROUP)
    q = q.reshape(b, l, SWA_KV_HEADS, SWA_GROUP, HEAD_DIM)

    pm = jnp.arange(N_META, dtype=jnp.float32)
    dist_mm = jnp.abs(pm[:, None] - pm[None, :])
    out_m = _attend_with_sinks(q[:, None, :N_META], k[:, None, :N_META], v[:, None, :N_META],
                               -slopes[:, :, None, None] * dist_mm, sinks)
    out_m = out_m.reshape(b, N_META, SWA_WIDTH)

    qr = q[:, N_META:].reshape(b, nb, BLOCK, SWA_KV_HEADS, SWA_GROUP, HEAD_DIM)

    def band(t):
        tr = t[:, N_META:]
        prev = jnp.pad(tr, ((0, 0), (BLOCK, 0), (0, 0), (0, 0)))[:, :s]
        bnd = jnp.concatenate([prev.reshape(b, nb, BLOCK, SWA_KV_HEADS, HEAD_DIM),
                               tr.reshape(b, nb, BLOCK, SWA_KV_HEADS, HEAD_DIM)], axis=2)
        meta = jnp.broadcast_to(t[:, None, :N_META], (b, nb, N_META, SWA_KV_HEADS, HEAD_DIM))
        return jnp.concatenate([meta, bnd], axis=2)

    kr, vr = band(k), band(v)
    a = jnp.arange(BLOCK)[:, None]
    c = jnp.arange(2 * BLOCK)[None, :]
    n = jnp.arange(nb)[:, None, None]
    ci = a // CHUNK
    cj = c // CHUNK - BLOCK // CHUNK
    band_ok = (cj <= ci) & (ci - cj < SWA_WIN_CHUNKS) & (n * BLOCK - BLOCK + c >= 0)
    band_dist = jnp.abs(a - c + BLOCK).astype(jnp.float32)
    meta_dist = (N_META + n * BLOCK + a - jnp.arange(N_META)[None, None, :]).astype(jnp.float32)
    dist = jnp.concatenate([meta_dist, jnp.broadcast_to(band_dist, (nb, BLOCK, 2 * BLOCK))], axis=-1)
    ok = jnp.concatenate([jnp.ones((nb, BLOCK, N_META), dtype=bool), band_ok], axis=-1)
    bias = jnp.where(ok[:, None, None], -slopes[None, :, :, None, None] * dist[:, None, None], NEG_INF)
    out_r = _attend_with_sinks(qr, kr, vr, bias, sinks).reshape(b, s, SWA_WIDTH)
    return jnp.concatenate([out_m, out_r], axis=1)

def _fox_branch(q, k, v, log_f):
    b, l = q.shape[0], q.shape[1]
    nblk = -(-l // BLOCK)
    lp = nblk * BLOCK
    c_key = jnp.cumsum(log_f, axis=1).transpose(0, 2, 1)
    qb = jnp.pad(q, ((0, 0), (0, lp - l), (0, 0), (0, 0))).reshape(
        b, nblk, BLOCK, FOX_HEADS, HEAD_DIM).transpose(1, 0, 2, 3, 4)
    cb = jnp.pad(c_key, ((0, 0), (0, 0), (0, lp - l))).reshape(
        b, FOX_HEADS, nblk, BLOCK).transpose(2, 0, 1, 3)
    pos = jnp.arange(lp).reshape(nblk, BLOCK)
    key_pos = jnp.arange(l)

    def block(args):
        qi, ci, pi = args
        logits = jnp.einsum('bthd,bshd->bhts', qi, k).astype(jnp.float32) * ATTN_SCALE
        logits = logits + (ci[..., :, None] - c_key[:, :, None, :])
        logits = jnp.where(pi[:, None] >= key_pos[None, :], logits, NEG_INF)
        probs = jax.nn.softmax(logits, axis=-1)
        return jnp.einsum('bhts,bshd->bthd', probs.astype(v.dtype), v)

    out = lax.map(block, (qb, cb, pos))
    return out.transpose(1, 0, 2, 3, 4).reshape(b, lp, FOX_WIDTH)[:, :l]

def setup_inputs(seed: int = 0) -> dict:
    key = jax.random.key(seed)
    ks = jax.random.split(key, 12)
    f32 = jnp.float32
    x = jax.random.normal(ks[0], (BATCH, SEQ, D_MODEL), f32)
    meta_tokens = jax.random.normal(ks[1], (N_META, D_MODEL), f32)
    g_pre = 1.0 + 0.1 * jax.random.normal(ks[2], (DEPTH, D_MODEL), f32)
    w_in = jax.random.normal(ks[3], (DEPTH, D_MODEL, D_IN), f32) * D_MODEL ** -0.5
    b_forget = 3.0 + 0.5 * jax.random.normal(ks[4], (DEPTH, FOX_HEADS), f32)
    b_gate = 0.1 * jax.random.normal(ks[5], (DEPTH, 2, D_MODEL), f32)
    sinks = 0.5 * jax.random.normal(ks[6], (DEPTH, SWA_KV_HEADS, SWA_GROUP), f32)
    w_up_swa = jax.random.normal(ks[7], (DEPTH, SWA_WIDTH, D_MODEL), f32) * SWA_WIDTH ** -0.5
    w_up_fox = jax.random.normal(ks[8], (DEPTH, FOX_WIDTH, D_MODEL), f32) * FOX_WIDTH ** -0.5
    w_out = jax.random.normal(ks[9], (DEPTH, D_MODEL, D_MODEL), f32) * D_MODEL ** -0.5
    g_post = 1.0 + 0.1 * jax.random.normal(ks[10], (DEPTH, D_MODEL), f32)
    return {"x": x, "meta_tokens": meta_tokens, "g_pre": g_pre, "w_in": w_in,
            "b_forget": b_forget, "b_gate": b_gate, "sinks": sinks,
            "w_up_swa": w_up_swa, "w_up_fox": w_up_fox, "w_out": w_out, "g_post": g_post}

def reference(x, meta_tokens, g_pre, w_in, b_forget, b_gate, sinks, w_up_swa, w_up_fox, w_out, g_post):
    b = x.shape[0]
    h = jnp.concatenate([jnp.broadcast_to(meta_tokens[None].astype(x.dtype), (b, N_META, D_MODEL)), x], axis=1)
    l = h.shape[1]
    split_idx = np.cumsum(IN_SPLITS)[:-1].tolist()
    for i in range(DEPTH):
        u = _rmsnorm(h, g_pre[i])
        qa, ka, va, za, qf, kf, vf, zf, ff, ga, gf = jnp.split(u @ w_in[i], split_idx, axis=-1)
        y_swa = _swa_branch(qa.reshape(b, l, SWA_Q_HEADS, HEAD_DIM),
                            ka.reshape(b, l, SWA_KV_HEADS, HEAD_DIM),
                            va.reshape(b, l, SWA_KV_HEADS, HEAD_DIM), sinks[i]) * jax.nn.silu(za)
        log_f = jax.nn.log_sigmoid((ff + b_forget[i]).astype(jnp.float32))
        y_fox = _fox_branch(qf.reshape(b, l, FOX_HEADS, HEAD_DIM),
                            kf.reshape(b, l, FOX_HEADS, HEAD_DIM),
                            vf.reshape(b, l, FOX_HEADS, HEAD_DIM), log_f) * jax.nn.silu(zf)
        merged = (jax.nn.sigmoid(ga + b_gate[i, 0]) * (y_swa @ w_up_swa[i])
                  + jax.nn.sigmoid(gf + b_gate[i, 1]) * (y_fox @ w_up_fox[i]))
        h = h + _rmsnorm(merged @ w_out[i], g_post[i])
    return h[:, N_META:]


_drawn_inputs = setup_inputs


def setup_inputs(seed=0):
    import zlib

    import numpy as np

    out = dict(_drawn_inputs(seed))
    spreads = {}
    factors = {}
    for name, (base, spread) in spreads.items():
        noise = np.random.default_rng([zlib.crc32(name.encode()), seed]).standard_normal(out[name].shape)
        drawn = base * np.exp(spread * noise) if base else spread * noise
        out[name] = __import__('jax').numpy.asarray(drawn.astype(out[name].dtype))
    for name, factor in factors.items():
        out[name] = (out[name] * factor).astype(out[name].dtype)
    return out
```

```python
from contextlib import ExitStack

import numpy as np

import concourse.bass as bass
from concourse import mybir

F32 = mybir.dt.float32
F32R = mybir.dt.float32r
BF16 = mybir.dt.bfloat16
ALU = mybir.AluOpType
ACT = mybir.ActivationFunctionType

P = 128
D_MODEL = 1024
SEQ = 1024
N_META = 16
LENGTH = SEQ + N_META
HEAD = 64
HEADS = 8
CHUNK = 64
KT = D_MODEL // P
NQ = SEQ // P
BANK = 512
EPS = 1e-6
SCALE = HEAD ** -0.5
MASK = -1e30
BIG = 3e38
PAIRS = 4
W_SWA = N_META + CHUNK + P
A_ROWS = N_META + CHUNK

COL_QA, COL_KA, COL_VA, COL_ZA = 0, 512, 640, 768
COL_QF, COL_KF, COL_VF, COL_ZF = 1280, 1792, 2304, 2816
COL_FF, COL_GA, COL_GF = 3328, 3336, 4360

ALL_TOKENS = [(0, 352), (352, 352), (704, 336)]
REAL_TOKENS = [(N_META, BANK), (N_META + BANK, BANK)]

W_RING = 2
X_RING = 6
U_RING = 6
S_RING = 3
T_RING = 2
PT_RING = 4

COPY_ENGINE = ("act", "dve", "dve", "dve", "act")


class Step:

    def __init__(self, kind, name=None, entry=None, c=None, t0=None, w=None, last=None, n=None, i=None, b=None,
                 d=None, half=None, t=None):
        self.kind = kind
        self.name = name
        self.entry = entry
        self.c = c
        self.t0 = t0
        self.w = w
        self.last = last
        self.n = n
        self.i = i
        self.b = b
        self.d = d
        self.half = half
        self.t = t
        self.k = None
        self.stage = None
        self.groups = []
        self.pieces = []
        self.first_piece = None
        self.last_piece = None
        self.n_tiles = None


def entries_of():
    out = [("f", 0), ("ks", 0), ("vs", 0), ("qs", 0)]
    for j in range(PAIRS):
        out += [("kf", j), ("vf", j), ("qf", j)]
        out += ([("qs", j + 1)] if j + 1 < PAIRS else []) + [("zs", j)] + ([("zf", j - 1)] if j else [])
    out += [("zf", PAIRS - 1)]
    for d in range(KT):
        out += [("ga", d), ("gf", d), ("up", d)]
    for half in range(2):
        out += [("out", d) for d in range(KT)]
    return out


def item_of(stage, t):
    if stage[0] == "s":
        tiles = [(0, A_ROWS), (A_ROWS, P)]
        pieces = [(0, W_SWA)]
    else:
        tiles = [(0, N_META)] + [(N_META + P * j, P) for j in range(t + 1)]
        n = t + 1
        k = -(-(N_META + P * n) // BANK)
        per = [n // k + (1 if x < n % k else 0) for x in range(k)]
        per.sort()
        pieces, at = [], 0
        for x, c in enumerate(per):
            w = P * c + (N_META if x == 0 else 0)
            pieces.append((at, w))
            at += w
    return tiles, pieces


def schedule():
    entries = entries_of()
    number = {}
    for e, name in enumerate(entries):
        number.setdefault(name, []).append(e)
    steps = []
    chunks = 0

    def project(name):
        nonlocal chunks
        out = []
        ranges = ALL_TOKENS if name[0] in ("f", "ks", "vs", "kf", "vf") else REAL_TOKENS
        for c, (t0, w) in enumerate(ranges):
            out.append(Step("project", name=name, entry=number[name][0], c=c, t0=t0, w=w,
                            last=c == len(ranges) - 1))
        if name[0] in ("vs", "vf"):
            out.append(Step("values", name=name))
        if name[0] == "f":
            out.append(Step("forget"))
        return out

    first = project(("f", 0))
    batches = [range(a, min(a + 2, NQ + 1)) for a in range(0, NQ + 1, 2)]

    def each(kind, b):
        return [Step(kind, n=n) for n in batches[b]] if b < len(batches) else []

    def roots(b):
        return [Step("u_root", t0=batches[b][0], w=len(batches[b]))] if b < len(batches) else []

    steps += each("u_square", 0) + roots(0) + each("u_square", 1)
    for b in range(len(batches)):
        steps += each("u_norm", b) + roots(b + 1) + each("u_square", b + 2)
        for st in each("u_split", b):
            steps.append(st)
            if st.n in (3, 6, 8):
                steps.append(first.pop(0))
    steps += first
    steps += project(("ks", 0))
    values_s = project(("vs", 0))
    steps += values_s[:-1] + project(("qs", 0)) + values_s[-1:]
    stages = [(b, j) for j in range(PAIRS) for b in ("s", "f")]
    items = [(st, t) for st in stages for t in range(NQ)]
    steps.append(Step("score", i=0))
    for s, (b, j) in enumerate(stages):
        fill = []
        if b == "s":
            names = [("kf", j), ("vf", j), ("qf", j)]
        else:
            names = ([("qs", j + 1)] if j + 1 < PAIRS else []) + [("zs", j)] + ([("zf", j - 1)] if j else [])
        slots = NQ - 1 if b == "s" else NQ - 2
        for name in names:
            fill += project(name)
        for t in range(NQ):
            i = s * NQ + t
            attend = Step("open", i=i)
            steps.append(attend)
            if i + 1 < len(items):
                steps.append(Step("score", i=i + 1))
            steps.append(Step("close", i=i, n=attend))
            steps += fill[len(fill) * t // slots:len(fill) * (t + 1) // slots] if t < slots else []
    steps += project(("zf", PAIRS - 1))
    steps.append(Step("split_y"))
    for d in range(KT):
        for b, g in enumerate(("ga", "gf")):
            for c in range(2):
                steps.append(Step("gate", b=b, d=d, c=c, entry=number[(g, d)][0], last=c == 1))
        if d == KT - 1:
            steps += [Step("split_m", d=x) for x in range(KT - 1)]
        for b in range(2):
            for c in range(2):
                steps.append(Step("up", b=b, d=d, c=c, entry=number[("up", d)][0], last=b == 1 and c == 1))
    steps.append(Step("split_m", d=KT - 1))
    for half in range(2):
        for d in range(KT):
            steps.append(Step("out", half=half, d=d, entry=number[("out", d)][half], last=True))
            if half == 1 and d % 2 == 0:
                steps.append(Step("finish", half=0, t=d // 2))
    steps += [Step("finish", half=1, t=t) for t in range(4)]

    n_piece = n_group = n_pgroup = n_chunk = n_out = n_norm = 0
    freed = {"act": 0, "dve": 0}
    for st in steps:
        if st.kind == "project":
            st.k = n_chunk
            n_chunk += 1
        elif st.kind == "values":
            if st.name[0] == "vf":
                tiles = [("f", x) for x in range(NQ + 1)]
                cut = [tiles[0:4], tiles[4:8], tiles[8:9]]
            else:
                a, b = [("a", x) for x in range(NQ)], [("b", x) for x in range(NQ)]
                cut = [a[0:4], a[4:8], b[0:4], b[4:8]]
            st.groups = []
            for tiles in cut:
                who = ("act", "dve")[n_group % 2]
                freed[who] += 1
                st.groups.append((n_group, who, freed[who], tiles))
                n_group += 1
        elif st.kind == "close":
            st.stage, st.t, st.groups, st.n_tiles = st.n.stage, st.n.t, st.n.groups, st.n.n_tiles
        elif st.kind == "score":
            st.stage, st.t = items[st.i]
            _, pieces = item_of(st.stage, st.t)
            st.pieces = [(h, x, c0, w) for x, (c0, w) in enumerate(pieces) for h in range(2)]
            st.first_piece = n_piece
            n_piece += len(st.pieces)
            st.last_piece = {h: max(n_piece - len(st.pieces) + y for y, q in enumerate(st.pieces) if q[0] == h)
                             for h in range(2)}
        elif st.kind == "open":
            st.stage, st.t = items[st.i]
            tiles, _ = item_of(st.stage, st.t)
            every = [(h, x, c0, w) for h in range(2) for x, (c0, w) in enumerate(tiles)]
            st.n_tiles = len(tiles)
            st.groups = []
            for a in range(0, len(every), 4):
                who = COPY_ENGINE[a // 4]
                freed[who] += 1
                st.groups.append((n_group, n_pgroup, who, freed[who], every[a:a + 4]))
                n_group += 1
                n_pgroup += 1
    owner = {}
    for st in steps:
        for g in groups_of(st):
            owner[g[0]] = (g[-3], g[-2])
    totals = dict(pieces=n_piece, groups=n_group, pgroups=n_pgroup, chunks=n_chunk,
                  freed=dict(freed), items=len(items))
    return entries, steps, owner, totals


def groups_of(st):
    return st.groups if st.kind in ("values", "open") else []


def build(nc, x, meta_tokens, g_pre, w_in, b_forget, b_gate, sinks, w_up_swa, w_up_fox, w_out, g_post,
          ident_in, const_in, rows_in, out):
    entries, steps, owner, totals = schedule()
    items_done_groups = {}
    for st in steps:
        if st.kind == "open":
            items_done_groups[st.i] = st.groups[-1]

    x_v = x.rearrange("b (n p) d -> (b n) p d", p=P)
    out_v = out.rearrange("b (n p) d -> (b n) p d", p=P)
    w_v = w_in.rearrange("o (k p) c -> p (o k) c", p=P)
    wo_v = w_out.rearrange("o (k p) c -> p (o k) c", p=P)
    wuf_v = w_up_fox.rearrange("o (k p) c -> p (o k) c", p=P)
    wus_v = w_up_swa.rearrange("o (g k p) c -> (o g) p k c", g=2, p=HEAD)
    neg_c_dram = nc.dram_tensor("neg_c_dram", (HEADS, LENGTH), F32).ap()

    with ExitStack() as ctx:
        def sb(name, shape, dt=F32, on=ctx):
            return on.enter_context(nc.sbuf_tensor(name, shape, dt))

        def sem(name):
            return ctx.enter_context(nc.semaphore(name))

        PS = ctx.enter_context(nc.psum_tensor("PS", [P, 8, BANK], F32))
        S_BANK, T_BANK, Y_BANK, PJ_BANK = 0, 3, 5, 6

        u_hi = sb("u_hi", [P, KT, LENGTH], F32R)
        u_lo = sb("u_lo", [P, KT, LENGTH], F32R)
        y = sb("y", [P, 2 * PAIRS, SEQ])
        w_raw = sb("w_raw", [P, W_RING, KT, P])
        w_hi = sb("w_hi", [P, W_RING, KT, P], F32R)
        w_lo = sb("w_lo", [P, W_RING, KT, P], F32R)
        ident = sb("ident", [P, P])
        half_bg = sb("half_bg", [P, 2, KT])
        stat = sb("stat", [P, 8, NQ + 1])

        att = ExitStack()
        const = sb("const", [P, 2 * P + HEADS * W_SWA], BF16, on=att)
        rows = sb("rows", [1, P + A_ROWS + HEADS * NQ * N_META], BF16, on=att)
        sink = sb("sink", [P, HEADS], on=att)
        neg_sink = sb("neg_sink", [P, HEADS], on=att)
        bf = sb("bf", [HEADS, 1], on=att)
        q_s = sb("q_s", [P, SEQ], on=att)
        q_f = sb("q_f", [P, SEQ], on=att)
        k_f = sb("k_f", [P, LENGTH], on=att)
        v_t = sb("v_t", [P, LENGTH], on=att)
        k_x = sb("k_x", [P, NQ, W_SWA], on=att)
        v_a = sb("v_a", [P, NQ, P], on=att)
        v_b = sb("v_b", [P, NQ, P], on=att)
        v_f = sb("v_f", [P, NQ + 1, P], on=att)
        neg_c = sb("neg_c", [P, 2, LENGTH], on=att)
        probs = sb("probs", [P, 2, 2, LENGTH], on=att)
        p_t = sb("p_t", [P, PT_RING, BANK], on=att)
        z_t = sb("z_t", [P, 2, BANK], on=att)
        neg_max = sb("neg_max", [P, 2, 2, 3], on=att)
        den = sb("den", [P, 2, 2], on=att)
        es = sb("es", [P, 2, 2], on=att)
        rec = sb("rec", [P, 2, 2], on=att)
        att.close()
        mrg = ExitStack()
        y_hi = sb("y_hi", [P, 2 * PAIRS, SEQ], F32R, on=mrg)
        y_lo = sb("y_lo", [P, 2 * PAIRS, SEQ], F32R, on=mrg)
        tanh_g = sb("tanh_g", [P, 2, 2, BANK], on=mrg)
        gated = sb("gated", [P, 2, 2, BANK], on=mrg)
        mrg.close()
        fin = ExitStack()
        o_t = sb("o_t", [P, 2, KT, BANK], on=fin)
        g_post_row = sb("g_post_row", [P, D_MODEL], on=fin)
        x_again = sb("x_again", [P, NQ, D_MODEL], on=fin)
        result = sb("result", [P, 2, D_MODEL], on=fin)
        squares2 = sb("squares2", [P, D_MODEL], on=fin)
        fin.close()

        ident_b = const[:, 0:P]
        causal = const[:, P:2 * P]
        alibi = const[:, 2 * P:].rearrange("p (h w) -> p h w", h=HEADS)
        ones_row = rows[0:1, 0:P]
        first_block_row = rows[0:1, P:P + A_ROWS]
        meta_far_row = rows[0:1, P + A_ROWS:].rearrange("o (h n m) -> o h n m", h=HEADS, n=NQ)

        x_t = [y[:, i, :] for i in range(X_RING)]
        squares = z_t[:, :, :].rearrange("p a b -> p (a b)")
        g_pre_row = y[:, X_RING, :]
        neg_c_rows = y[0:HEADS, 5:7, :].rearrange("p a b -> p (a b)")[:, 0:LENGTH]
        v_a_t = y[:, 7, 0:NQ * A_ROWS].rearrange("p (n w) -> p n w", n=NQ)
        f_x = probs[0:HEADS, 0, 0, :]
        f_e = probs[0:HEADS, 0, 1, :]
        f_ones = probs[0:HEADS, 1, 0, :]
        f_r = probs[0:HEADS, 1, 1, :]
        m_hi, m_lo = u_hi, u_lo

        x_loaded = [sem(f"x_loaded{i}") for i in range(X_RING)]
        w_loaded = [sem(f"w_loaded{i}") for i in range(W_RING)]
        const_loaded = sem("const_loaded")
        g_pre_loaded = sem("g_pre_loaded")
        ident_loaded = sem("ident_loaded")
        neg_c_stored = sem("neg_c_stored")
        neg_c_loaded = sem("neg_c_loaded")
        again_loaded = sem("again_loaded")
        g_post_loaded = sem("g_post_loaded")
        out_stored = [sem(f"out_stored{i}") for i in range(2)]
        act_chain = sem("act_chain")
        dve_chain = sem("dve_chain")
        x_squared = sem("x_squared")
        x_rooted = sem("x_rooted")
        var_ready = sem("var_ready")
        x_normed = sem("x_normed")
        cleared = sem("cleared")
        u_transposed = sem("u_transposed")
        u_hi_ready = sem("u_hi_ready")
        u_ready = sem("u_ready")
        w_hi_ready = sem("w_hi_ready")
        w_ready = sem("w_ready")
        chunk_done = sem("chunk_done")
        chunk_drained = sem("chunk_drained")
        z_tanh = sem("z_tanh")
        z_used = sem("z_used")
        f_step = sem("f_step")
        f_back = sem("f_back")
        neg_c_ready = sem("neg_c_ready")
        swa_keys_ready = sem("swa_keys_ready")
        swa_values_ready = sem("swa_values_ready")
        transposed = sem("transposed")
        group_freed = {"act": sem("group_freed_act"), "dve": sem("group_freed_dve")}
        scored = sem("scored")
        logits_ready = sem("logits_ready")
        exp_done = sem("exp_done")
        normed = sem("normed")
        group_used = sem("group_used")
        y_copied = sem("y_copied")
        y_hi_ready = sem("y_hi_ready")
        y_split = sem("y_split")
        gate_done = sem("gate_done")
        gate_tanh = sem("gate_tanh")
        up_done = sem("up_done")
        up_gated = sem("up_gated")
        m_ready = sem("m_ready")
        m_hi_ready = sem("m_hi_ready")
        m_split = sem("m_split")
        out_done = sem("out_done")
        out_copied = sem("out_copied")
        natural_done = sem("natural_done")
        out_squared = sem("out_squared")
        out_var = sem("out_var")
        out_rooted = sem("out_rooted")
        result_ready = sem("result_ready")

        block = ctx.enter_context(nc.Block())

        def w_parts(e):
            kind, j = entries[e]
            slot = w_raw[:, e % W_RING]
            if kind in ("qs", "zs"):
                base = COL_QA if kind == "qs" else COL_ZA
                return [(slot[:, :, g * HEAD:(g + 1) * HEAD],
                         w_v[:, :, base + (j + PAIRS * g) * HEAD:base + (j + PAIRS * g + 1) * HEAD])
                        for g in range(2)]
            if kind == "up":
                cols = slice(j * P, (j + 1) * P)
                return [(slot[g * HEAD:(g + 1) * HEAD, 0:PAIRS, :], wus_v[g][:, :, cols]) for g in range(2)] + [
                    (slot[:, PAIRS:KT, :], wuf_v[:, :, cols])]
            if kind == "out":
                return [(slot, wo_v[:, :, j * P:(j + 1) * P])]
            base = {"f": COL_FF, "ks": COL_KA, "vs": COL_VA, "qf": COL_QF, "kf": COL_KF, "vf": COL_VF, "zf": COL_ZF,
                    "ga": COL_GA, "gf": COL_GF}[kind] + j * P
            return [(slot, w_v[:, :, base:base + P])]

        slot_count = [0] * W_RING
        w_target = []
        for e in range(len(entries)):
            slot_count[e % W_RING] += 16 * len(w_parts(e))
            w_target.append(slot_count[e % W_RING])

        entry_end, z_number, q_chunk, values_ready, values_chunk = {}, {}, {}, {}, {}
        exps_until, exps = [0], 0
        for st in steps:
            if st.kind == "project":
                entry_end[st.entry] = (chunk_done, st.k + 1)
                kind, j = st.name
                if kind in ("zs", "zf"):
                    z_number[st.k] = len(z_number)
                if kind in ("qs", "qf"):
                    q_chunk[(kind[1], j)] = st.k
                if kind in ("vs", "vf"):
                    values_chunk[st.name] = st.k
            elif st.kind == "gate":
                entry_end[st.entry] = (gate_done, 4 * st.d + 2 * st.b + st.c + 1)
            elif st.kind == "up":
                entry_end[st.entry] = (up_done, 4 * st.d + 2 * st.b + st.c + 1)
            elif st.kind == "out":
                entry_end[st.entry] = (out_done, 8 * st.half + st.d + 1)
            elif st.kind == "score":
                exps_until.append(exps_until[-1] + (4 if st.stage[0] == "s" else 2))
            elif st.kind == "values":
                values_ready[(st.name[0][1], st.name[1])] = {who: v for _, who, v, _ in st.groups}
        scores = {st.i: st for st in steps if st.kind == "score"}

        def starts_entry(st):
            return (st.kind == "out" or st.kind in ("project", "gate") and st.c == 0
                    or st.kind == "up" and st.b == 0 and st.c == 0)

        def bank4(bank, r):
            return PS[:, bank, :].rearrange("p (k t) -> p k t", k=4)[:, :, 0:r]

        def natural(n):
            return PS[:, 4 + 2 * (n % 2):6 + 2 * (n % 2), :].rearrange("p a b -> p (a b)")

        def values_copy(g, tiles):
            what, n0 = tiles[0]
            r = A_ROWS if what == "a" else P
            dst = {"a": v_a, "b": v_b, "f": v_f}[what][0:r, n0:n0 + len(tiles), :]
            return dst, PS[0:r, T_BANK + g % T_RING, 0:P * len(tiles)].rearrange("p (n d) -> p n d", n=len(tiles))

        last_score_of_stage = {}
        for st in steps:
            if st.kind == "score":
                last_score_of_stage[st.stage] = st

        CONST_LOADS = 6
        KEYS_COPIES, VALUES_COPIES = NQ + 3, NQ + 2

        @block.sync
        def _(sp):
            late = [False]

            def load_w(e):
                if e >= W_RING:
                    sp.wait_ge(w_ready, e - W_RING + 1)
                for dst, src in w_parts(e):
                    sp.dma_start(dst, src).then_inc(w_loaded[e % W_RING], 16)

            def load_x(n):
                if n >= X_RING:
                    sp.wait_ge(u_transposed, 2 * (n - X_RING) + 2)
                if n == 0:
                    sp.dma_start(x_t[0][0:N_META, :], meta_tokens).then_inc(x_loaded[0], 16)
                else:
                    sp.dma_start(x_t[n % X_RING], x_v[n - 1]).then_inc(x_loaded[n % X_RING], 16)

            with nc.allow_non_contiguous_dma(reason="small constants"):
                for n in range(4):
                    load_x(n)
                load_w(0)
                load_x(4)
                load_x(5)
                load_w(1)
                for n in range(6, NQ + 1):
                    load_x(n)
                for e in range(W_RING, len(entries)):
                    kind, j = entries[e - W_RING]
                    if kind == "qs" and j == 0:
                        sp.wait_ge(neg_c_ready, 1)
                        sp.dma_start(neg_c_dram, neg_c_rows).then_inc(neg_c_stored, 16)
                        sp.wait_ge(neg_c_stored, 16)
                    if (kind == "qs" and j == 0) or kind == "kf" and j > 0:
                        if j:
                            sp.wait_ge(logits_ready, last_score_of_stage[("f", j - 1)].last_piece[1] + 1)
                        for h in range(2):
                            sp.dma_start(neg_c[:, h, :], neg_c_dram[2 * j + h:2 * j + h + 1, :].to_broadcast(
                                [P, LENGTH])).then_inc(neg_c_loaded, 16)
                    if kind == "out" and j == 0 and entries[e][0] == "out" and not late[0]:
                        late[0] = True
                        sp.wait_ge(m_ready, 2 * KT)
                        sp.wait_ge(up_done, 4 * KT)
                        sp.dma_start(g_post_row[:, :], g_post.to_broadcast([P, D_MODEL])).then_inc(g_post_loaded, 16)
                        sp.dma_start(x_again[:, :, :], x_v.rearrange("n p d -> p n d")).then_inc(again_loaded, 16)
                    load_w(e)

        @block.gpsimd
        def _(pool):
            def split_lo(e):
                s = e % W_RING
                pool.wait_ge(w_hi_ready, e + 1)
                nc.gpsimd.tensor_tensor(w_lo[:, s], w_raw[:, s], w_hi[:, s].bitcast(F32),
                                        ALU.subtract).then_inc(w_ready, 1)

            split_lo(0)
            for st in steps:
                if starts_entry(st) and st.entry + 1 < len(entries):
                    split_lo(st.entry + 1)
                if st.kind == "project" and st.name[0] in ("ks", "vs") and st.last:
                    pool.wait_ge(chunk_drained, st.k + 1)
                    keys = st.name[0] == "ks"
                    src = k_f if keys else v_t
                    dst = k_x if keys else v_a_t
                    real = src[:, N_META:].rearrange("p (n w) -> p n w", n=NQ)
                    done = swa_keys_ready if keys else swa_values_ready
                    nc.gpsimd.memset(dst[:, 0, N_META:A_ROWS], 0.0).then_inc(done, 1)
                    nc.gpsimd.tensor_copy(dst[:, 1:, N_META:A_ROWS], real[:, 0:NQ - 1, CHUNK:P]).then_inc(done, 1)
                    for n in range(NQ):
                        nc.gpsimd.tensor_copy(dst[:, n, 0:N_META], src[:, 0:N_META]).then_inc(done, 1)
                    if keys:
                        nc.gpsimd.tensor_copy(dst[:, :, A_ROWS:], real).then_inc(done, 1)
                if st.kind == "up" and st.b == 1:
                    pool.wait_ge(up_gated, 4 * st.d + 3 + st.c)
                    nc.gpsimd.tensor_tensor(y[:, st.d, st.c * BANK:(st.c + 1) * BANK], gated[:, 0, st.c, :],
                                            gated[:, 1, st.c, :], ALU.add).then_inc(m_ready, 1)

        @block.scalar
        def _(act):
            chain = [0]

            def split_hi(e):
                s = e % W_RING
                act.wait_ge(w_loaded[s], w_target[e])
                if e >= W_RING:
                    act.wait_ge(*entry_end[e - W_RING])
                nc.scalar.activation(w_hi[:, s], w_raw[:, s], ACT.Copy).then_inc(w_hi_ready, 1)

            def load_const(dst, src, signal=const_loaded):
                act.dma_start(dst, src).then_inc(signal, 16)

            with nc.allow_non_contiguous_dma(reason="small constants"):
                load_const(g_pre_row, g_pre.to_broadcast([P, D_MODEL]), g_pre_loaded)
                load_const(ident[:, :], ident_in, ident_loaded)
                load_const(const[:, :], const_in.bitcast(BF16))
                load_const(rows[:, :], rows_in.bitcast(BF16))
                load_const(sink[:, :], sinks.rearrange("o g h -> o (g h)").to_broadcast([P, HEADS]))
                load_const(bf[:, :], b_forget.rearrange("o h -> h o"))
                for b in range(2):
                    load_const(half_bg[:, b, :], b_gate[0, b].rearrange("(k p) -> p k", p=P))

            def store(n):
                act.wait_ge(result_ready, n + 1)
                act.dma_start(out_v[n], result[:, n % 2, :]).then_inc(out_stored[n % 2], 16)

            split_hi(0)
            for st in steps:
                if starts_entry(st) and st.entry + 1 < len(entries):
                    split_hi(st.entry + 1)
                if st.kind == "u_square":
                    n = st.n
                    r = N_META if n == 0 else P
                    act.wait_ge(x_loaded[n % X_RING], 16 * (n // X_RING + 1))
                    if n:
                        act.wait_ge(x_squared, n)
                    else:
                        act.wait_ge(cleared, 1)
                    nc.scalar.activation(squares[0:r, :], x_t[n % X_RING][0:r, :], ACT.Square,
                                         accum_out=stat[0:r, 0, n:n + 1]).then_inc(x_squared, 1)
                elif st.kind == "u_root":
                    cols = slice(st.t0, st.t0 + st.w)
                    act.wait_ge(var_ready, st.t0 // 2 + 1)
                    nc.scalar.activation(stat[:, 2, cols], stat[:, 1, cols], ACT.Sqrt).then_inc(x_rooted, 1)
                elif st.kind == "u_split":
                    n = st.n
                    r = N_META if n == 0 else P
                    c0 = 0 if n == 0 else N_META + (n - 1) * P
                    for g in range(2 * n, 2 * n + 2):
                        k0 = 4 * (g % 2)
                        act.wait_ge(u_transposed, g + 1)
                        nc.scalar.activation(u_hi[:, k0:k0 + 4, c0:c0 + r], bank4(g % U_RING, r),
                                             ACT.Copy).then_inc(u_hi_ready, 1)
                elif st.kind == "forget":
                    act.wait_ge(f_step, 1)
                    nc.scalar.activation(f_e, f_e, ACT.Exp, scale=-1.0).then_inc(f_back, 1)
                    act.wait_ge(f_back, 1)
                    nc.scalar.activation(f_e, f_e, ACT.Ln, bias=1.0).then_inc(f_back, 1)
                elif st.kind == "project" and st.name[0] in ("zs", "zf"):
                    act.wait_ge(chunk_done, st.k + 1)
                    z_no = z_number[st.k]
                    if z_no >= 2:
                        act.wait_ge(z_used, z_no - 1)
                    nc.scalar.activation(z_t[:, st.c, :], PS[:, PJ_BANK + st.k % 2, :], ACT.Tanh,
                                         scale=0.5).then_inc(z_tanh, 1)
                elif st.kind == "values":
                    for g, who, v, tiles in st.groups:
                        if who == "act":
                            act.wait_ge(transposed, g + 1)
                            dst, src = values_copy(g, tiles)
                            nc.scalar.activation(dst, src, ACT.Copy).then_inc(group_freed["act"], 1)
                elif st.kind == "score":
                    b = st.i % 2
                    for h in range(2):
                        act.wait_ge(logits_ready, st.last_piece[h] + 1)
                        x_last = max(q[1] for q in st.pieces)
                        width = max(q[2] + q[3] for q in st.pieces)
                        bias = neg_max[:, b, h, x_last:x_last + 1]
                        nc.scalar.activation(probs[:, b, h, 0:width], probs[:, b, h, 0:width], ACT.Exp, bias=bias,
                                             scale=-1.0, accum_out=den[:, b, h:h + 1]).then_inc(exp_done, 1)
                        if st.stage[0] == "s":
                            hh = st.stage[1] + PAIRS * h
                            nc.scalar.activation(es[:, b, h:h + 1], sink[:, hh:hh + 1], ACT.Exp,
                                                 bias=bias).then_inc(exp_done, 1)
                elif st.kind in ("open", "close"):
                    for g, pg, who, v, tiles in st.groups[:2] if st.kind == "open" else st.groups[2:]:
                        if who == "act":
                            act.wait_ge(transposed, g + 1)
                            if pg >= PT_RING:
                                act.wait_ge(group_used, pg - PT_RING + 1)
                            nc.scalar.activation(p_t[:, pg % PT_RING, 0:P * len(tiles)],
                                                 PS[:, T_BANK + g % T_RING, 0:P * len(tiles)],
                                                 ACT.Copy).then_inc(group_freed["act"], 1)
                elif st.kind == "split_y":
                    act.wait_ge(group_used, totals["pgroups"])
                    act.wait_ge(z_used, 4 * PAIRS)
                    for s in range(2 * PAIRS):
                        nc.scalar.activation(y_hi[:, s, :], y[:, s, :], ACT.Copy).then_inc(y_hi_ready, 1)
                elif st.kind == "gate":
                    k = 4 * st.d + 2 * st.b + st.c
                    act.wait_ge(gate_done, k + 1)
                    if st.d:
                        act.wait_ge(up_gated, 4 * (st.d - 1) + 2 * st.b + st.c + 1)
                    nc.scalar.activation(tanh_g[:, st.b, st.c, :], PS[:, 2 * st.b + st.c, :], ACT.Tanh, scale=0.5,
                                         bias=half_bg[:, st.b, st.d:st.d + 1]).then_inc(gate_tanh, 1)
                elif st.kind == "split_m":
                    if st.d == 0:
                        act.wait_ge(gate_done, 4 * KT)
                    act.wait_ge(m_ready, 2 * st.d + 2)
                    nc.scalar.activation(m_hi[:, st.d, 0:SEQ], y[:, st.d, :], ACT.Copy,
                                         scale=0.5).then_inc(m_hi_ready, 1)
                elif st.kind == "out":
                    k = 8 * st.half + st.d
                    act.wait_ge(out_done, k + 1)
                    nc.scalar.activation(o_t[:, st.half, st.d, :], PS[:, k % 4, :], ACT.Copy).then_inc(out_copied, 1)
                elif st.kind == "finish":
                    n = 4 * st.half + st.t
                    act.wait_ge(natural_done, n + 1)
                    if n:
                        act.wait_ge(out_squared, n)
                    nc.scalar.activation(squares2[:, :], natural(n), ACT.Square,
                                         accum_out=stat[:, 4, n:n + 1]).then_inc(out_squared, 1)
                    act.wait_ge(out_var, n + 1)
                    nc.scalar.activation(stat[:, 6, n:n + 1], stat[:, 5, n:n + 1], ACT.Sqrt).then_inc(out_rooted, 1)
                    if n:
                        store(n - 1)

            store(NQ - 1)
            act.wait_ge(out_stored[0], 16 * NQ // 2)
            act.wait_ge(out_stored[1], 16 * NQ // 2)

        @block.vector
        def _(dve):
            chain = [0]

            def link(ins):
                chain[0] += 1
                ins.then_inc(dve_chain, 1)
                dve.wait_ge(dve_chain, chain[0])

            def root(base, cols):
                a, s, t = (stat[:, base + x, cols] for x in (1, 2, 3))
                link(nc.vector.reciprocal(t, s))
                link(nc.vector.tensor_tensor(t, t, a, ALU.mult))
                link(nc.vector.tensor_tensor(t, t, s, ALU.add))
                link(nc.vector.tensor_scalar(t, t, 0.5, None, ALU.mult))
                link(nc.vector.reciprocal(t, t))
                return t

            def norm(st):
                b = st.i % 2
                dve.wait_ge(exp_done, exps_until[st.i + 1])
                if st.stage[0] == "s":
                    link(nc.vector.tensor_tensor(den[:, b, :], den[:, b, :], es[:, b, :], ALU.add))
                link(nc.vector.reciprocal(rec[:, b, :], den[:, b, :]))
                width = max(q[2] + q[3] for q in st.pieces)
                for h in range(2):
                    nc.vector.tensor_scalar(probs[:, b, h, 0:width], probs[:, b, h, 0:width],
                                            rec[:, b, h:h + 1], None, ALU.mult).then_inc(normed, 1)

            nc.vector.memset(stat[:, 0, :], 1.0).then_inc(cleared, 1)
            nc.vector.memset(f_ones, 1.0).then_inc(cleared, 1)
            for st in steps:
                if st.kind == "u_root":
                    cols = slice(st.t0, st.t0 + st.w)
                    dve.wait_ge(x_squared, st.t0 + st.w)
                    nc.vector.tensor_scalar(stat[:, 1, cols], stat[:, 0, cols], 1.0 / D_MODEL, EPS, ALU.mult,
                                            ALU.add).then_inc(var_ready, 1)
                    dve.wait_ge(x_rooted, st.t0 // 2 + 1)
                    root(0, cols)
                elif st.kind == "u_norm":
                    n = st.n
                    r = N_META if n == 0 else P
                    xs = x_t[n % X_RING][0:r, :]
                    if n == 0:
                        dve.wait_ge(g_pre_loaded, 16)
                    nc.vector.scalar_tensor_tensor(out=xs, in0=xs, scalar=stat[0:r, 3, n:n + 1],
                                                   in1=g_pre_row[0:r, :], op0=ALU.mult,
                                                   op1=ALU.mult).then_inc(x_normed, 1)
                elif st.kind == "u_split":
                    n = st.n
                    r = N_META if n == 0 else P
                    c0 = 0 if n == 0 else N_META + (n - 1) * P
                    for g in range(2 * n, 2 * n + 2):
                        k0 = 4 * (g % 2)
                        dve.wait_ge(u_hi_ready, g + 1)
                        nc.vector.tensor_tensor(u_lo[:, k0:k0 + 4, c0:c0 + r], bank4(g % U_RING, r),
                                                u_hi[:, k0:k0 + 4, c0:c0 + r].bitcast(F32),
                                                ALU.subtract).then_inc(u_ready, 1)
                elif st.kind == "project":
                    kind = st.name[0]
                    src = PS[:, PJ_BANK + st.k % 2, 0:st.w]
                    dve.wait_ge(chunk_done, st.k + 1)
                    if kind == "f":
                        dve.wait_ge(const_loaded, 16 * CONST_LOADS)
                        nc.vector.tensor_scalar(f_x[:, st.t0:st.t0 + st.w], src[0:HEADS, :], bf[:, 0:1], None,
                                                ALU.add).then_inc(chunk_drained, 1)
                    elif kind in ("qs", "qf"):
                        dst = q_s if kind == "qs" else q_f
                        nc.vector.tensor_scalar(dst[:, st.t0 - N_META:st.t0 - N_META + st.w], src, SCALE, None,
                                                ALU.mult).then_inc(chunk_drained, 1)
                    elif kind in ("ks", "kf"):
                        if kind == "kf" and st.name[1] == 0 and st.c == 0:
                            dve.wait_ge(swa_keys_ready, KEYS_COPIES)
                        nc.vector.tensor_copy(k_f[:, st.t0:st.t0 + st.w], src).then_inc(chunk_drained, 1)
                    elif kind in ("vs", "vf"):
                        if kind == "vf" and st.name[1] == 0 and st.c == 0:
                            dve.wait_ge(swa_values_ready, VALUES_COPIES)
                        nc.vector.tensor_copy(v_t[:, st.t0:st.t0 + st.w], src).then_inc(chunk_drained, 1)
                    else:
                        slot = st.name[1] + (0 if kind == "zs" else PAIRS)
                        yy = y[:, slot, st.c * BANK:(st.c + 1) * BANK]
                        zz = z_t[:, st.c, :]
                        dve.wait_ge(z_tanh, z_number[st.k] + 1)
                        ins = nc.vector.scalar_tensor_tensor(out=zz, in0=zz, scalar=1.0, in1=src, op0=ALU.add,
                                                             op1=ALU.mult)
                        ins.then_inc(chunk_drained, 1)
                        dve.wait_ge(chunk_drained, st.k + 1)
                        nc.vector.scalar_tensor_tensor(out=yy, in0=zz, scalar=0.5, in1=yy, op0=ALU.mult,
                                                       op1=ALU.mult).then_inc(z_used, 1)
                elif st.kind == "forget":
                    nc.vector.tensor_scalar(half_bg[:, :, :], half_bg[:, :, :], 0.5, None, ALU.mult
                                            ).then_inc(cleared, 1)
                    nc.vector.tensor_scalar(neg_sink[:, :], sink[:, :], -1.0, None, ALU.mult).then_inc(cleared, 1)
                    dve.wait_ge(cleared, 4)
                    dve.wait_ge(chunk_drained, 3)
                    nc.vector.scalar_tensor_tensor(out=f_e, in0=f_x, scalar=-1.0, in1=f_x, op0=ALU.mult,
                                                   op1=ALU.max).then_inc(f_step, 1)
                    link(nc.vector.tensor_scalar(f_x, f_x, -1.0, 0.0, ALU.mult, ALU.max))
                    dve.wait_ge(f_back, 2)
                    link(nc.vector.tensor_tensor(f_r, f_x, f_e, ALU.add))
                    nc.vector.tensor_tensor_scan(neg_c_rows, f_ones, f_r, 0.0, ALU.mult,
                                                 ALU.add).then_inc(neg_c_ready, 1)
                elif st.kind == "values":
                    for g, who, v, tiles in st.groups:
                        if who == "dve":
                            dve.wait_ge(transposed, g + 1)
                            dst, src = values_copy(g, tiles)
                            nc.vector.tensor_copy(dst, src).then_inc(group_freed["dve"], 1)
                elif st.kind == "score":
                    b = st.i % 2
                    swa = st.stage[0] == "s"
                    if st.i >= 2:
                        dve.wait_ge(transposed, items_done_groups[st.i - 2][0] + 1)
                    if not swa and st.t == 0:
                        dve.wait_ge(neg_c_loaded, 32 * (st.stage[1] + 1))
                    for y_, (h, x_, c0, w) in enumerate(st.pieces):
                        k = st.first_piece + y_
                        hh = st.stage[1] + PAIRS * h
                        dve.wait_ge(scored, k + 1)
                        if x_:
                            dve.wait_ge(logits_ready, k - 1)
                        init = neg_max[:, b, h, x_ - 1:x_] if x_ else (neg_sink[:, hh:hh + 1] if swa else BIG)
                        in1 = alibi[:, hh, :] if swa else neg_c[:, h, c0:c0 + w]
                        nc.vector.tensor_tensor_reduce(probs[:, b, h, c0:c0 + w],
                                                       PS[:, S_BANK + k % S_RING, 0:w], in1, -1.0, init,
                                                       ALU.add, ALU.min,
                                                       neg_max[:, b, h, x_:x_ + 1]).then_inc(logits_ready, 1)
                    if st.i == 0:
                        norm(st)
                elif st.kind in ("open", "close"):
                    for g, pg, who, v, tiles in st.groups[:2] if st.kind == "open" else st.groups[2:]:
                        if who == "dve":
                            dve.wait_ge(transposed, g + 1)
                            if pg >= PT_RING:
                                dve.wait_ge(group_used, pg - PT_RING + 1)
                            nc.vector.tensor_copy(p_t[:, pg % PT_RING, 0:P * len(tiles)],
                                                  PS[:, T_BANK + g % T_RING, 0:P * len(tiles)]
                                                  ).then_inc(group_freed["dve"], 1)
                    if st.kind == "close":
                        if st.i + 1 < totals["items"]:
                            norm(scores[st.i + 1])
                        dve.wait_ge(group_used, st.groups[-1][1] + 1)
                        slot = st.stage[1] + (0 if st.stage[0] == "s" else PAIRS)
                        nc.vector.tensor_copy(y[:, slot, st.t * P:(st.t + 1) * P],
                                              PS[:, Y_BANK, 0:P]).then_inc(y_copied, 1)
                elif st.kind == "split_y":
                    for s in range(2 * PAIRS):
                        dve.wait_ge(y_hi_ready, s + 1)
                        nc.vector.tensor_tensor(y_lo[:, s, :], y[:, s, :], y_hi[:, s, :].bitcast(F32),
                                                ALU.subtract).then_inc(y_split, 1)
                elif st.kind == "up":
                    k = 4 * st.d + 2 * st.b + st.c
                    dve.wait_ge(up_done, k + 1)
                    dve.wait_ge(gate_tanh, k + 1)
                    if st.d:
                        dve.wait_ge(m_ready, 2 * (st.d - 1) + st.c + 1)
                    nc.vector.scalar_tensor_tensor(out=gated[:, st.b, st.c, :], in0=tanh_g[:, st.b, st.c, :],
                                                   scalar=1.0, in1=PS[:, 4 + 2 * st.b + st.c, :], op0=ALU.add,
                                                   op1=ALU.mult).then_inc(up_gated, 1)
                elif st.kind == "split_m":
                    dve.wait_ge(m_hi_ready, st.d + 1)
                    nc.vector.scalar_tensor_tensor(out=m_lo[:, st.d, 0:SEQ], in0=y[:, st.d, :], scalar=0.5,
                                                   in1=m_hi[:, st.d, 0:SEQ].bitcast(F32), op0=ALU.mult,
                                                   op1=ALU.subtract).then_inc(m_split, 1)
                elif st.kind == "finish":
                    n = 4 * st.half + st.t
                    dve.wait_ge(out_squared, n + 1)
                    nc.vector.tensor_scalar(stat[:, 5, n:n + 1], stat[:, 4, n:n + 1], 1.0 / D_MODEL, EPS, ALU.mult,
                                            ALU.add).then_inc(out_var, 1)
                    dve.wait_ge(out_rooted, n + 1)
                    t = root(4, slice(n, n + 1))
                    if n == 0:
                        dve.wait_ge(g_post_loaded, 16)
                    if n >= 2:
                        dve.wait_ge(out_stored[n % 2], 16 * (n // 2))
                    link(nc.vector.scalar_tensor_tensor(out=result[:, n % 2, :], in0=natural(n), scalar=t,
                                                        in1=g_post_row[:, :], op0=ALU.mult, op1=ALU.mult))
                    if n == 0:
                        dve.wait_ge(again_loaded, 16)
                    nc.vector.tensor_tensor(result[:, n % 2, :], result[:, n % 2, :], x_again[:, n, :],
                                            ALU.add).then_inc(result_ready, 1)

        @block.tensor
        def _(pe):
            def three(dst, e, k, hi, lo, first, last):
                s = e % W_RING
                pe.matmul(dst, w_hi[:, s, k, :], hi, start=first, stop=False)
                pe.matmul(dst, w_hi[:, s, k, :], lo, start=False, stop=False)
                return pe.matmul(dst, w_lo[:, s, k, :], hi, start=False, stop=last)

            def free_bank_of(g):
                if g >= T_RING:
                    who, v = owner[g - T_RING]
                    pe.wait_ge(group_freed[who], v)

            pe.wait_ge(ident_loaded, 16)
            for st in steps:
                if st.kind in ("project", "gate", "up", "out"):
                    pe.wait_ge(w_ready, st.entry + 1)
                if st.kind == "u_norm":
                    n = st.n
                    r = N_META if n == 0 else P
                    pe.wait_ge(x_normed, n + 1)
                    for g in range(2 * n, 2 * n + 2):
                        if g >= U_RING:
                            pe.wait_ge(u_ready, g - U_RING + 1)
                        for j in range(4):
                            k = 4 * (g % 2) + j
                            ins = pe.transpose(PS[:, g % U_RING, j * P:j * P + r],
                                               x_t[n % X_RING][0:r, k * P:(k + 1) * P], ident[0:r, 0:r])
                        ins.then_inc(u_transposed, 1)
                elif st.kind == "project":
                    tiles = -(-(st.t0 + st.w - N_META) // P) + 1
                    pe.wait_ge(u_ready, 2 * tiles)
                    if st.k >= 2:
                        pe.wait_ge(chunk_drained, st.k - 1)
                    dst = PS[:, PJ_BANK + st.k % 2, 0:st.w]
                    tok = slice(st.t0, st.t0 + st.w)
                    for k in range(KT):
                        ins = three(dst, st.entry, k, u_hi[:, k, tok], u_lo[:, k, tok], k == 0, k == KT - 1)
                    ins.then_inc(chunk_done, 1)
                elif st.kind == "values":
                    swa = st.name[0] == "vs"
                    pe.wait_ge(chunk_drained, values_chunk[st.name] + 1)
                    if swa:
                        pe.wait_ge(swa_values_ready, VALUES_COPIES)
                    for g, who, v, tiles in st.groups:
                        free_bank_of(g)
                        for j, (what, n) in enumerate(tiles):
                            if what == "a":
                                src, r = v_a_t[:, n, :], A_ROWS
                            elif what == "b" or n:
                                m = n if what == "b" else n - 1
                                src, r = v_t[:, N_META + m * P:N_META + (m + 1) * P], P
                            else:
                                src, r = v_t[:, 0:P], P
                            ins = pe.transpose(PS[0:r, T_BANK + g % T_RING, j * P:(j + 1) * P], src, ident[:, :])
                        ins.then_inc(transposed, 1)
                elif st.kind == "score":
                    swa = st.stage[0] == "s"
                    pe.wait_ge(chunk_drained, q_chunk[st.stage] + 1)
                    pe.wait_ge(u_ready, 2 * (NQ + 1))
                    if swa:
                        pe.wait_ge(swa_keys_ready, KEYS_COPIES)
                    q = q_s if swa else q_f
                    for y_, (h, x_, c0, w) in enumerate(st.pieces):
                        k = st.first_piece + y_
                        hh = st.stage[1] + PAIRS * h
                        if k >= S_RING:
                            pe.wait_ge(logits_ready, k - S_RING + 1)
                        bank = PS[:, S_BANK + k % S_RING, :]
                        rows_ = slice(h * HEAD, (h + 1) * HEAD)
                        keys = k_x[rows_, st.t, :] if swa else k_f[rows_, c0:c0 + w]
                        more = swa or c0 + w == N_META + (st.t + 1) * P
                        ins = pe.matmul(bank[:, 0:w], q[rows_, st.t * P:(st.t + 1) * P], keys, start=True,
                                        stop=not more)
                        if swa and st.t == 0:
                            ins = pe.matmul(bank[:, 0:A_ROWS], ones_row, first_block_row, start=False, stop=True)
                        elif swa:
                            ins = pe.matmul(bank[:, 0:N_META], ones_row, meta_far_row[:, hh, st.t, :], start=False,
                                            stop=True)
                        elif more:
                            ins = pe.matmul(bank[:, w - P:w], ident_b, causal, start=False, stop=True)
                        ins.then_inc(scored, 1)
                elif st.kind in ("open", "close"):
                    b = st.i % 2
                    swa = st.stage[0] == "s"

                    def transposes(n):
                        g, pg, who, v, tiles = st.groups[n]
                        free_bank_of(g)
                        for j, (h, x_, c0, w) in enumerate(tiles):
                            pe.wait_ge(normed, 2 * st.i + h + 1)
                            w = P if w == N_META else w
                            ins = pe.transpose(PS[0:w, T_BANK + g % T_RING, j * P:(j + 1) * P],
                                               probs[:, b, h, c0:c0 + w], ident[:, :])
                        ins.then_inc(transposed, 1)

                    def values(n):
                        g, pg, who, v, tiles = st.groups[n]
                        pe.wait_ge(group_freed[who], v)
                        for j, (h, x_, c0, w) in enumerate(tiles):
                            cols = slice(h * HEAD, (h + 1) * HEAD)
                            vv = (v_a, v_b)[x_][0:w, st.t, cols] if swa else v_f[0:w, x_, cols]
                            ins = pe.matmul(PS[h * HEAD:(h + 1) * HEAD, Y_BANK, 0:P], vv,
                                            p_t[0:w, pg % PT_RING, j * P:(j + 1) * P], start=x_ == 0,
                                            stop=x_ == st.n_tiles - 1)
                        ins.then_inc(group_used, 1)

                    if st.kind == "open":
                        for n in range(len(st.groups[:2])):
                            transposes(n)
                        continue
                    if st.i:
                        pe.wait_ge(y_copied, st.i)
                    if st.t == 0:
                        for w_, v_ in values_ready[("s", 0) if swa else st.stage].items():
                            pe.wait_ge(group_freed[w_], v_)
                    for n in range(len(st.groups)):
                        values(n)
                        if n + 2 < len(st.groups):
                            transposes(n + 2)
                elif st.kind == "gate":
                    if st.d == 0 and st.b == 0 and st.c == 0:
                        pe.wait_ge(chunk_drained, totals["chunks"])
                        pe.wait_ge(y_copied, totals["items"])
                    if st.d:
                        pe.wait_ge(gate_tanh, 4 * (st.d - 1) + 2 * st.b + st.c + 1)
                    tok = slice(N_META + st.c * BANK, N_META + (st.c + 1) * BANK)
                    for k in range(KT):
                        ins = three(PS[:, 2 * st.b + st.c, :], st.entry, k, u_hi[:, k, tok], u_lo[:, k, tok],
                                    k == 0, k == KT - 1)
                    ins.then_inc(gate_done, 1)
                elif st.kind == "up":
                    if st.d == 0:
                        pe.wait_ge(y_split, PAIRS * (st.b + 1))
                    if st.d:
                        pe.wait_ge(up_gated, 4 * (st.d - 1) + 2 * st.b + st.c + 1)
                    tok = slice(st.c * BANK, (st.c + 1) * BANK)
                    for j in range(PAIRS):
                        k = PAIRS * st.b + j
                        ins = three(PS[:, 4 + 2 * st.b + st.c, :], st.entry, k, y_hi[:, k, tok], y_lo[:, k, tok],
                                    j == 0, j == PAIRS - 1)
                    ins.then_inc(up_done, 1)
                elif st.kind == "out":
                    k_ = 8 * st.half + st.d
                    if k_ == 0:
                        pe.wait_ge(gate_tanh, 4 * KT)
                        pe.wait_ge(m_split, KT)
                    if k_ >= 4:
                        pe.wait_ge(out_copied, k_ - 3)
                    tok = slice(st.half * BANK, (st.half + 1) * BANK)
                    for k in range(KT):
                        ins = three(PS[:, k_ % 4, :], st.entry, k, m_hi[:, k, tok], m_lo[:, k, tok], k == 0,
                                    k == KT - 1)
                    ins.then_inc(out_done, 1)
                elif st.kind == "finish":
                    n = 4 * st.half + st.t
                    if st.t == 0:
                        pe.wait_ge(out_copied, 8 * (st.half + 1))
                    if n == 0:
                        pe.wait_ge(up_gated, 4 * KT)
                    if n >= 2:
                        pe.wait_ge(result_ready, n - 1)
                    for d in range(KT):
                        ins = pe.transpose(PS[:, 4 + 2 * (n % 2) + d // 4, (d % 4) * P:(d % 4 + 1) * P],
                                           o_t[:, st.half, d, st.t * P:(st.t + 1) * P], ident[:, :])
                    ins.then_inc(natural_done, 1)


_INS = ["x", "meta_tokens", "g_pre", "w_in", "b_forget", "b_gate", "sinks", "w_up_swa", "w_up_fox", "w_out",
        "g_post"]


def constants():
    def bf16_bits(a):
        return (np.ascontiguousarray(a, np.float32).view(np.uint32) >> 16).astype(np.uint16)

    slopes = 2.0 ** -np.arange(1, HEADS + 1)
    ident = np.eye(P, dtype=np.float32)
    a, c = np.arange(P)[:, None], np.arange(P)[None, :]
    causal = np.where(c <= a, 0.0, MASK)
    meta = N_META + a - np.arange(N_META)[None, :]
    back = a - (np.arange(CHUNK)[None, :] - CHUNK)
    dist = np.concatenate([meta, back, np.abs(a - c)], axis=1)
    ok = np.concatenate([np.ones((P, N_META), bool), np.broadcast_to(a < CHUNK, (P, CHUNK)),
                         (c // CHUNK) <= (a // CHUNK)], axis=1)
    alibi = np.where(ok[:, None, :], -slopes[None, :, None] * dist[:, None, :], MASK)
    const = bf16_bits(np.concatenate([ident, causal, alibi.reshape(P, -1)], axis=1))
    first = np.where(np.arange(A_ROWS) < N_META, 0.0, MASK)
    far = np.broadcast_to((-slopes[:, None] * P * np.arange(NQ)[None, :])[:, :, None], (HEADS, NQ, N_META))
    rows = bf16_bits(np.concatenate([np.ones(P), first, far.reshape(-1)])[None, :])
    return {"ident": ident, "const": const, "rows": rows}


def kernel(**inputs):
    import concourse.bacc as _bacc
    from concourse.bass_utils import run_bass_kernel_spmd as _run

    nc = _bacc.Bacc("TRN2", target_bir_lowering=False, num_devices=1)
    arrays, args = {}, []
    data = {n: np.ascontiguousarray(inputs[n]) for n in _INS}
    data.update(constants())
    for name, a in data.items():
        arrays[f"in_{name}_dram"] = a
        args.append(nc.dram_tensor(f"in_{name}_dram", a.shape, mybir.dt.from_np(a.dtype), kind="ExternalInput").ap())
    args.append(nc.dram_tensor("out_dram", (1, SEQ, D_MODEL), F32, kind="ExternalOutput").ap())
    build(nc, *args)
    return _run(nc, [arrays], core_ids=[0]).results[0]["out_dram"]
```

```python
from contextlib import ExitStack

import numpy as np

import concourse.bass as bass
from concourse import mybir

F32 = mybir.dt.float32
F32R = mybir.dt.float32r
BF16 = mybir.dt.bfloat16
ALU = mybir.AluOpType
ACT = mybir.ActivationFunctionType

P = 128
D_MODEL = 1024
SEQ = 1024
N_META = 16
LENGTH = SEQ + N_META
HEAD = 64
HEADS = 8
CHUNK = 64
KT = D_MODEL // P
NQ = SEQ // P
BANK = 512
EPS = 1e-6
SCALE = HEAD ** -0.5
MASK = -1e30
BIG = 3e38
PAIRS = 4
W_SWA = N_META + CHUNK + P
W_SLOTS = 7
A_ROWS = N_META + CHUNK

COL_QA, COL_KA, COL_VA, COL_ZA = 0, 512, 640, 768
COL_QF, COL_KF, COL_VF, COL_ZF = 1280, 1792, 2304, 2816
COL_FF, COL_GA, COL_GF = 3328, 3336, 4360

ALL_TOKENS = [(0, 352), (352, 352), (704, 336)]
EARLY_TOKENS = [(0, N_META + 2 * P)] + [(N_META + 2 * P * x, 2 * P) for x in range(1, 4)]
REAL_TOKENS = [(N_META + 2 * P * x, 2 * P) for x in range(4)]

OUT_GROUPS = [(0, 4), (4, 2), (6, 2)]

U_RING = 6

FILL = {("s", 11): (2, 1, 1, 1, 1, 1, 2, 2), ("f", 12): (2, 2, 2, 2, 1, 1, 1, 1), ("f", 8): (1,) * NQ}
POOL_GAINS = (3, 4, 5, 6, 7, 8)
S_RING = 3
T_RING = 2
PT_RING = 4

COPY_ENGINE = ("act", "dve", "dve", "dve", "act")


class Step:

    def __init__(self, kind, name=None, entry=None, c=None, t0=None, w=None, last=None, n=None, i=None, b=None,
                 d=None, half=None, t=None, k=None):
        self.kind = kind
        self.name = name
        self.entry = entry
        self.c = c
        self.t0 = t0
        self.w = w
        self.last = last
        self.n = n
        self.i = i
        self.b = b
        self.d = d
        self.half = half
        self.t = t
        self.k = k
        self.stage = None
        self.groups = []
        self.pieces = []
        self.first_piece = None
        self.last_piece = None
        self.n_tiles = None


def entries_of():
    out = [("f", 0), ("ks", 0), ("vs", 0), ("qs", 0)]
    for j in range(PAIRS):
        out += [("kf", j), ("qf", j), ("vf", j)]
        out += ([("qs", j + 1)] if j + 1 < PAIRS else []) + [("zs", j)] + ([("zf", j - 1)] if j else [])
    out += [("zf", PAIRS - 1)]
    for d in range(KT):
        out += [("ga", d), ("gf", d), ("up", d)]
    for _ in OUT_GROUPS:
        out += [("out", d) for d in range(KT)]
    return out


def item_of(stage, t):
    if stage[0] == "s":
        tiles = [(0, A_ROWS), (A_ROWS, P)]
        pieces = [(0, W_SWA)]
    else:
        tiles = [(0, N_META)] + [(N_META + P * j, P) for j in range(t + 1)]
        n = t + 1
        k = -(-(N_META + P * n) // BANK)
        per = [n // k + (1 if x < n % k else 0) for x in range(k)]
        per.sort()
        pieces, at = [], 0
        for x, c in enumerate(per):
            w = P * c + (N_META if x == 0 else 0)
            pieces.append((at, w))
            at += w
    return tiles, pieces


def schedule():
    entries = entries_of()
    number = {}
    for e, name in enumerate(entries):
        number.setdefault(name, []).append(e)
    steps = []
    chunks = 0

    def project(name):
        nonlocal chunks
        out = []
        early = name[0] in ("f", "ks")
        ranges = EARLY_TOKENS if early else ALL_TOKENS if name[0] in ("vs", "kf", "vf") else REAL_TOKENS
        for c, (t0, w) in enumerate(ranges):
            out.append(Step("project", name=name, entry=number[name][0], c=c, t0=t0, w=w,
                            last=c == len(ranges) - 1))
            if not early:
                out.append(Step("drain", n=out[-1]))
        if name[0] in ("vs", "vf"):
            out.append(Step("values", name=name))
        return out

    early = {4 + 2 * c: project(("f", 0))[c] for c in range(4)}
    early.update({5 + 2 * c: project(("ks", 0))[c] for c in range(4)})
    drains = {}
    steps.append(Step("u_square", n=0))
    for m in range(NQ + 4):
        tile = m <= NQ
        if tile:
            steps.append(Step("u_var", n=m))
        if m + 1 <= NQ:
            steps.append(Step("u_square", n=m + 1))
        if 1 <= m <= NQ + 1:
            steps.append(Step("u_copy", n=m - 1))
        subs = [Step("u_lo", n=m - 2, t=g) for g in range(2)] if 2 <= m <= NQ + 2 else []
        steps += subs[:1]
        if tile:
            steps.append(Step("u_newton", n=m))
        steps += subs[1:]
        if tile:
            steps.append(Step("u_norm", n=m))
        if m - 1 in early:
            steps.append(Step("drain", n=early[m - 1]))
        if m in early:
            steps.append(early[m])
        if m in (1, 3):
            steps.append(Step("split_w", entry=m // 2))
    steps.append(Step("drain", n=early[NQ + 3]))
    steps.append(Step("forget"))
    values_s = project(("vs", 0))
    steps += values_s[:-1] + project(("qs", 0)) + values_s[-1:]
    stages = [(b, j) for j in range(PAIRS) for b in ("s", "f")]
    items = [(st, t) for st in stages for t in range(NQ)]
    head = Step("score", i=0)
    steps += [head, Step("piece", n=head), Step("norm", n=head)]
    for s, (b, j) in enumerate(stages):
        fill = []
        if b == "s":
            names = [("kf", j), ("qf", j), ("vf", j)]
        else:
            names = ([("qs", j + 1)] if j + 1 < PAIRS else []) + [("zs", j)] + ([("zf", j - 1)] if j else [])
        for name in names:
            for x in project(name):
                if x.kind == "drain":
                    fill[-1].append(x)
                else:
                    fill.append([x])
        for t in range(NQ):
            i = s * NQ + t
            attend = Step("open", i=i)
            steps.append(attend)
            if i + 1 < len(items):
                following = Step("score", i=i + 1)
                steps += [following, Step("piece", n=following)]
            else:
                following = None
            steps.append(Step("close", i=i, n=attend))
            if following:
                steps.append(Step("norm", n=following))
            steps.append(Step("y_copy", i=i, n=attend))
            fills = FILL[(b, len(fill))]
            for unit in fill[sum(fills[:t]):sum(fills[:t + 1])]:
                steps += unit
    steps += project(("zf", PAIRS - 1))
    steps.append(Step("split_y"))
    for d in range(KT):
        for b, g in enumerate(("ga", "gf")):
            for c in range(2):
                steps.append(Step("gate", b=b, d=d, c=c, entry=number[(g, d)][0], last=c == 1))
        ups = [[Step("up", b=b, d=d, c=c, entry=number[("up", d)][0], last=b == 1 and c == 1) for b in range(2)]
               for c in range(2)]
        if d < KT - 1:
            steps += ups[0] + ups[1]
        else:
            splits = [[Step("split_m", d=x, c=c, k=KT * c + x) for x in range(KT)] for c in range(2)]
            steps += splits[0][:3] + ups[0] + splits[0][3:] + ups[1] + splits[1]
    for g, (n0, n) in enumerate(OUT_GROUPS):
        for d in range(KT):
            steps.append(Step("out", half=g, d=d, t0=n0 * P, w=n * P, entry=number[("out", d)][g], last=True,
                              k=KT * g + d))
            if g and d % 2 and d // 2 < OUT_GROUPS[g - 1][1]:
                steps += [Step("natural", n=OUT_GROUPS[g - 1][0] + d // 2, half=part) for part in range(2)]
            if g and d % 2 == 0 and 1 <= d // 2 <= OUT_GROUPS[g - 1][1]:
                steps.append(Step("finish", n=OUT_GROUPS[g - 1][0] + d // 2 - 1))
            if g == 2 and d == 0:
                steps.append(Step("finish", n=3))
            if g == len(OUT_GROUPS) - 1 and d == KT - 2:
                steps += [Step("natural", n=x, half=0) for x in range(n0, n0 + n)]
    steps += [Step("natural", n=x, half=1) for x in range(n0, n0 + n)] + [
        Step("finish", n=x) for x in range(n0, n0 + n)]

    timed, seen = [], 2
    for st in steps:
        if st.entry is not None and st.kind != "split_w" and (st.entry != 1 or st.last):
            while seen < len(entries) and seen <= st.entry + (2 if st.kind == "out" else 1):
                timed.append(Step("split_w", entry=seen))
                seen += 1
        timed.append(st)
    steps = timed

    n_piece = n_group = n_pgroup = n_chunk = n_natural = 0
    freed = {"act": 0, "dve": 0}
    for st in steps:
        if st.kind == "project":
            st.k = n_chunk
            n_chunk += 1
        elif st.kind == "natural":
            st.k = n_natural
            n_natural += 1
        elif st.kind == "values":
            if st.name[0] == "vf":
                tiles = [("f", x) for x in range(NQ + 1)]
                cut = [tiles[0:4], tiles[4:8], tiles[8:9]]
            else:
                a, b = [("a", x) for x in range(NQ)], [("b", x) for x in range(NQ)]
                cut = [a[0:4], a[4:8], b[0:4], b[4:8]]
            st.groups = []
            for tiles in cut:
                who = ("act", "dve")[n_group % 2]
                freed[who] += 1
                st.groups.append((n_group, who, freed[who], tiles))
                n_group += 1
        elif st.kind in ("close", "y_copy"):
            st.stage, st.t, st.groups, st.n_tiles = st.n.stage, st.n.t, st.n.groups, st.n.n_tiles
        elif st.kind == "score":
            st.stage, st.t = items[st.i]
            _, pieces = item_of(st.stage, st.t)
            st.pieces = [(h, x, c0, w) for x, (c0, w) in enumerate(pieces) for h in range(2)]
            st.first_piece = n_piece
            n_piece += len(st.pieces)
            st.last_piece = {h: max(n_piece - len(st.pieces) + y for y, q in enumerate(st.pieces) if q[0] == h)
                             for h in range(2)}
        elif st.kind == "open":
            st.stage, st.t = items[st.i]
            tiles, _ = item_of(st.stage, st.t)
            every = [(h, x, c0, w) for h in range(2) for x, (c0, w) in enumerate(tiles)]
            st.n_tiles = len(tiles)
            st.groups = []
            for a in range(0, len(every), 4):
                who = COPY_ENGINE[a // 4]
                freed[who] += 1
                st.groups.append((n_group, n_pgroup, who, freed[who], every[a:a + 4]))
                n_group += 1
                n_pgroup += 1
    owner = {}
    for st in steps:
        for g in groups_of(st):
            owner[g[0]] = (g[-3], g[-2])
    totals = dict(pieces=n_piece, groups=n_group, pgroups=n_pgroup, chunks=n_chunk,
                  freed=dict(freed), items=len(items))
    woven, waiting = [], []
    for st in steps:
        if st.kind == "piece":
            score = st.n
            pieces = [Step("piece", i=score.i, n=score, t=y) for y in range(len(score.pieces))]
            now = len(pieces) if score.i == 0 else S_RING
            woven += pieces[:now]
            waiting = pieces[now:]
        elif st.kind == "close":
            for g in range(len(st.groups)):
                woven.append(Step("pv", i=st.i, n=st, t=g))
                woven += waiting[:1]
                waiting = waiting[1:]
            woven += waiting
        elif st.kind != "score":
            woven.append(st)
    steps = woven
    return entries, steps, owner, totals


def groups_of(st):
    return st.groups if st.kind in ("values", "open") else []


def build(nc, x, meta_tokens, g_pre, w_in, b_forget, b_gate, sinks, w_up_swa, w_up_fox, w_out, g_post,
          ident_in, const_in, rows_in, out):
    entries, steps, owner, totals = schedule()
    items_done_groups = {}
    for st in steps:
        if st.kind == "open":
            items_done_groups[st.i] = st.groups[-1]

    x_v = x.rearrange("b (n p) d -> (b n) p d", p=P)
    out_v = out.rearrange("b (n p) d -> (b n) p d", p=P)
    w_v = w_in.rearrange("o (k p) c -> p (o k) c", p=P)
    wo_v = w_out.rearrange("o (k p) c -> p (o k) c", p=P)
    wuf_v = w_up_fox.rearrange("o (k p) c -> p (o k) c", p=P)
    wus_v = w_up_swa.rearrange("o (g k p) c -> (o g) p k c", g=2, p=HEAD)
    neg_c_dram = nc.dram_tensor("neg_c_dram", (HEADS, LENGTH), F32).ap()

    with ExitStack() as ctx:
        def sb(name, shape, dt=F32, on=ctx):
            return on.enter_context(nc.sbuf_tensor(name, shape, dt))

        def sem(name):
            return ctx.enter_context(nc.semaphore(name))

        PS = ctx.enter_context(nc.psum_tensor("PS", [P, 8, BANK], F32))
        S_BANK, T_BANK, Y_BANK, PJ_BANK = 0, 3, 5, 6

        once = ExitStack()
        u_hi = sb("u_hi", [P, KT, LENGTH], F32R)
        u_lo = sb("u_lo", [P, KT, LENGTH], F32R)
        y = sb("y", [P, 2 * PAIRS, SEQ], on=once)
        w_raw_slots = sb("w_raw_slots", [P, 2, KT, P], on=once)
        once.close()
        y_r = sb("y_r", [P, 2 * PAIRS, SEQ], F32R)
        w_low_slots = sb("w_low_slots", [P, 2, KT, P], F32R)
        w_hi_slots = sb("w_hi_slots", [P, 2, KT, P], F32R)
        ident = sb("ident", [P, P])
        half_bg = sb("half_bg", [P, 2, KT])
        stat = sb("stat", [P, 10, NQ + 1])

        att = ExitStack()
        const = sb("const", [P, 2 * P + HEADS * W_SWA], BF16, on=att)
        rows = sb("rows", [1, P + A_ROWS + HEADS * NQ], BF16, on=att)
        sink = sb("sink", [P, HEADS], on=att)
        neg_sink = sb("neg_sink", [P, HEADS], on=att)
        bf = sb("bf", [HEADS, 1], on=att)
        q_s = sb("q_s", [P, SEQ], on=att)
        first = ExitStack()
        w_raw_third = sb("w_raw_third", [P, KT, P], on=first)
        first.close()
        qq_f = sb("qq_f", [P, 2, SEQ], F32R, on=att)
        q_lo = sb("q_lo", [P, SEQ], F32R, on=att)
        kk_f = sb("kk_f", [P, 2, LENGTH], F32R, on=att)
        v_t = sb("v_t", [P, LENGTH], on=att)
        k_x = sb("k_x", [P, NQ, W_SWA], on=att)
        v_a = sb("v_a", [P, NQ, P], on=att)
        v_b = sb("v_b", [P, NQ, P], on=att)
        v_f = sb("v_f", [P, NQ + 1, P], on=att)
        neg_c = sb("neg_c", [P, 2, LENGTH], on=att)
        probs = sb("probs", [P, 2, 2, LENGTH], on=att)
        p_t = sb("p_t", [P, PT_RING, BANK], on=att)
        z_t = sb("z_t", [P, BANK], on=att)
        neg_max = sb("neg_max", [P, 2, 2, 3], on=att)
        den = sb("den", [P, 2, 2], on=att)
        es = sb("es", [P, 2, 2], on=att)
        rec = sb("rec", [P, 2, 2], on=att)
        att.close()
        mrg = ExitStack()
        y_hi = sb("y_hi", [P, 2 * PAIRS, SEQ], F32R, on=mrg)
        y_lo = sb("y_lo", [P, 2 * PAIRS, SEQ], F32R, on=mrg)
        tanh_g = sb("tanh_g", [P, 2, 2, BANK], on=mrg)
        gated = sb("gated", [P, 2, 2, BANK], on=mrg)
        mrg.close()
        fin = ExitStack()
        o_t = sb("o_t", [P, 2, KT, BANK], on=fin)
        g_post_row = sb("g_post_row", [P, D_MODEL], on=fin)
        x_again = sb("x_again", [P, NQ, D_MODEL], on=fin)
        result = sb("result", [P, 2, D_MODEL], on=fin)
        squares2 = sb("squares2", [P, D_MODEL], on=fin)
        fin.close()

        ident_b = const[:, 0:P]
        causal = const[:, P:2 * P]
        alibi = const[:, 2 * P:].rearrange("p (h w) -> p h w", h=HEADS)
        ones_row = rows[0:1, 0:P]
        first_block_row = rows[0:1, P:P + A_ROWS]
        meta_far_row = rows[0:1, P + A_ROWS:].rearrange("o (h n) -> o h n", h=HEADS)

        x_t = [v_a[:, :, :].rearrange("p a b -> p (a b)")] + [y[:, i, :] for i in range(NQ)]
        squares = neg_c[:, :, :].rearrange("p a b -> p (a b)")[:, 0:D_MODEL]
        g_pre_row = v_b[:, :, :].rearrange("p a b -> p (a b)")
        k_s = y[:, 0:2, :].rearrange("p a b -> p (a b)")[:, 0:LENGTH]
        neg_c_rows = y[0:HEADS, 5:7, :].rearrange("p a b -> p (a b)")[:, 0:LENGTH]
        v_a_t = y[:, 7, 0:NQ * A_ROWS].rearrange("p (n w) -> p n w", n=NQ)
        f_x = probs[0:HEADS, 0, 0, :]
        f_e = probs[0:HEADS, 0, 1, :]
        f_ones = probs[0:HEADS, 1, 0, :]
        f_r = probs[0:HEADS, 1, 1, :]
        m_hi, m_lo = u_hi, u_lo
        w_raw = [w_raw_slots[:, 0], w_raw_slots[:, 1], w_raw_third[:, :, :]]
        w_low = [w_low_slots[:, 0], w_low_slots[:, 1], qq_f[:, 0, :].rearrange("p (k c) -> p k c", k=KT)]
        w_hi = [w_hi_slots[:, 0], w_hi_slots[:, 1], qq_f[:, 1, :].rearrange("p (k c) -> p k c", k=KT)]
        for x in range(4):
            w_raw.append(y[:, :, 2 * P * x:2 * P * x + P])
            w_low.append(y_r[:, :, 2 * P * x:2 * P * x + P])
            w_hi.append(y_r[:, :, 2 * P * x + P:2 * P * (x + 1)])

        x_loaded = [sem(f"x_loaded{i}") for i in range(NQ + 1)]
        w_loaded = [sem(f"w_loaded{i}") for i in range(W_SLOTS)]
        const_loaded = sem("const_loaded")
        g_pre_loaded = sem("g_pre_loaded")
        ident_loaded = sem("ident_loaded")
        neg_c_stored = sem("neg_c_stored")
        neg_c_loaded = sem("neg_c_loaded")
        again_loaded = [sem(f"again_loaded{i}") for i in range(NQ)]
        g_post_loaded = sem("g_post_loaded")
        out_stored = [sem(f"out_stored{i}") for i in range(2)]
        dve_chain = sem("dve_chain")
        fox_hi_ready = sem("fox_hi_ready")
        fox_lo_ready = sem("fox_lo_ready")
        fox_stacked = {"kf": sem("fox_keys_stacked"), "qf": sem("fox_queries_stacked")}
        x_squared = sem("x_squared")
        x_rooted = sem("x_rooted")
        var_ready = sem("var_ready")
        x_gained = sem("x_gained")
        x_normed = sem("x_normed")
        x_newton = sem("x_newton")
        cleared = sem("cleared")
        u_transposed = sem("u_transposed")
        u_hi_ready = sem("u_hi_ready")
        u_ready = sem("u_ready")
        w_hi_ready = sem("w_hi_ready")
        w_ready = {"pool": sem("w_ready_pool"), "dve": sem("w_ready_dve")}
        chunk_done = sem("chunk_done")
        chunk_drained = sem("chunk_drained")
        z_tanh = sem("z_tanh")
        z_used = sem("z_used")
        f_step = sem("f_step")
        f_back = sem("f_back")
        neg_c_ready = sem("neg_c_ready")
        swa_keys_ready = sem("swa_keys_ready")
        swa_values_ready = sem("swa_values_ready")
        transposed = sem("transposed")
        group_freed = {"act": sem("group_freed_act"), "dve": sem("group_freed_dve")}
        scored = sem("scored")
        logits_ready = sem("logits_ready")
        exp_done = sem("exp_done")
        normed = sem("normed")
        group_used = sem("group_used")
        y_copied = sem("y_copied")
        y_hi_ready = sem("y_hi_ready")
        y_split = sem("y_split")
        gate_done = sem("gate_done")
        gate_tanh = sem("gate_tanh")
        up_done = sem("up_done")
        up_gated = sem("up_gated")
        m_ready = sem("m_ready")
        m_hi_ready = sem("m_hi_ready")
        m_split = sem("m_split")
        out_done = sem("out_done")
        out_copied = sem("out_copied")
        natural_done = sem("natural_done")
        out_squared = sem("out_squared")
        out_var = sem("out_var")
        out_rooted = sem("out_rooted")
        result_scaled = sem("result_scaled")
        result_ready = {"pool": sem("result_ready_pool"), "dve": sem("result_ready_dve")}

        block = ctx.enter_context(nc.Block())

        first_out = len(entries) - KT * len(OUT_GROUPS)

        def slot_of(e):
            if e < 3:
                return e
            if e < first_out:
                return (e + 1) % 2
            return ((first_out + 1) % 2, first_out % 2, 3, 4, 5, 6)[(e - first_out) % 6]

        def w_parts(e):
            kind, j = entries[e]
            slot = w_raw[slot_of(e)]
            if kind in ("qs", "zs"):
                base = COL_QA if kind == "qs" else COL_ZA
                return [(slot[:, :, g * HEAD:(g + 1) * HEAD],
                         w_v[:, :, base + (j + PAIRS * g) * HEAD:base + (j + PAIRS * g + 1) * HEAD])
                        for g in range(2)]
            if kind == "up":
                cols = slice(j * P, (j + 1) * P)
                return [(slot[g * HEAD:(g + 1) * HEAD, 0:PAIRS, :], wus_v[g][:, :, cols]) for g in range(2)] + [
                    (slot[:, PAIRS:KT, :], wuf_v[:, :, cols])]
            if kind == "out":
                return [(slot, wo_v[:, :, j * P:(j + 1) * P])]
            base = {"f": COL_FF, "ks": COL_KA, "vs": COL_VA, "qf": COL_QF, "kf": COL_KF, "vf": COL_VF, "zf": COL_ZF,
                    "ga": COL_GA, "gf": COL_GF}[kind] + j * P
            return [(slot, w_v[:, :, base:base + P])]

        slot_count = [0] * W_SLOTS
        slot_user = [None] * W_SLOTS
        w_target, last_in_slot = [], []
        for e in range(len(entries)):
            s = slot_of(e)
            slot_count[s] += 16 * len(w_parts(e))
            w_target.append(slot_count[s])
            last_in_slot.append(slot_user[s])
            slot_user[s] = e

        entry_end, z_number, q_chunk, values_ready, values_chunk = {}, {}, {}, {}, {}
        exps_until = [0]
        fox_chunk, fox_chunks = {}, {}
        drained, plain = {}, 0
        for st in steps:
            if st.kind == "project":
                entry_end[st.entry] = (chunk_done, st.k + 1)
                kind, j = st.name
                if kind in ("kf", "qf"):
                    fox_chunk[st.k] = len(fox_chunk)
                    fox_chunks[st.name] = 2 * len(fox_chunk)
                    drained[st.k] = (fox_lo_ready, 2 * len(fox_chunk))
                else:
                    plain += 1
                    drained[st.k] = (chunk_drained, plain)
                if kind in ("zs", "zf"):
                    z_number[st.k] = len(z_number)
                if kind in ("qs", "qf"):
                    q_chunk[(kind[1], j)] = st.k
                if kind in ("vs", "vf"):
                    values_chunk[st.name] = st.k
            elif st.kind == "gate":
                entry_end[st.entry] = (gate_done, 4 * st.d + 2 * st.b + st.c + 1)
            elif st.kind == "up":
                entry_end[st.entry] = (up_done, 4 * st.d + 2 * st.c + st.b + 1)
            elif st.kind == "out":
                entry_end[st.entry] = (out_done, st.k + 1)
            elif st.kind == "piece" and st.t == 0:
                exps_until.append(exps_until[-1] + (4 if st.n.stage[0] == "s" else 2))
            elif st.kind == "values":
                values_ready[(st.name[0][1], st.name[1])] = {who: v for _, who, v, _ in st.groups}

        by_pool = first_out + KT

        def split_done(e):
            return (w_ready["pool"], e + 1) if e < by_pool else (w_ready["dve"], e - by_pool + 1)

        def groups_now(st):
            return st.groups[:2] if st.kind == "open" else st.n.groups[st.t + 2:st.t + 3]

        def bank4(bank, r):
            return PS[:, bank, :].rearrange("p (k t) -> p k t", k=4)[:, :, 0:r]

        def fox_part(st, h):
            part = slice(h * HEAD, (h + 1) * HEAD)
            if st.name[0] == "kf":
                return part, kk_f[part, h, st.t0:st.t0 + st.w]
            return part, qq_f[part, h, st.t0 - N_META:st.t0 - N_META + st.w]

        def natural(n):
            return PS[:, 4 + 2 * (n % 2):6 + 2 * (n % 2), :].rearrange("p a b -> p (a b)")

        def values_copy(g, tiles):
            what, n0 = tiles[0]
            r = A_ROWS if what == "a" else P
            dst = {"a": v_a, "b": v_b, "f": v_f}[what][0:r, n0:n0 + len(tiles), :]
            return dst, PS[0:r, T_BANK + g % T_RING, 0:P * len(tiles)].rearrange("p (n d) -> p n d", n=len(tiles))

        last_score_of_stage = {}
        for st in steps:
            if st.kind == "piece":
                last_score_of_stage[st.n.stage] = st.n

        CONST_LOADS = 6
        KEYS_COPIES, VALUES_COPIES = NQ + 3, NQ + 2

        @block.sync
        def _(sp):
            def load_const(dst, src):
                sp.dma_start(dst, src).then_inc(const_loaded, 16)

            def load_w(e):
                if last_in_slot[e] is not None:
                    sp.wait_ge(*entry_end[last_in_slot[e]])
                elif e >= first_out:
                    sp.wait_ge(m_split, KT if slot_of(e) < 5 else 2 * KT)
                for dst, src in w_parts(e):
                    sp.dma_start(dst, src).then_inc(w_loaded[slot_of(e)], 16)

            def load_x(n):
                if n == 0:
                    sp.dma_start(x_t[0][0:N_META, :], meta_tokens).then_inc(x_loaded[0], 16)
                else:
                    sp.dma_start(x_t[n], x_v[n - 1]).then_inc(x_loaded[n], 16)

            with nc.allow_non_contiguous_dma(reason="small constants"):
                for n in range(3):
                    load_x(n)
                load_w(0)
                for n in range(3, 6):
                    load_x(n)
                load_w(1)
                for n in range(6, NQ + 1):
                    load_x(n)
                load_const(const[:, :], const_in.bitcast(BF16))
                load_const(rows[:, :], rows_in.bitcast(BF16))
                load_const(sink[:, :], sinks.rearrange("o g h -> o (g h)").to_broadcast([P, HEADS]))
                load_const(bf[:, :], b_forget.rearrange("o h -> h o"))
                for b in range(2):
                    load_const(half_bg[:, b, :], b_gate[0, b].rearrange("(k p) -> p k", p=P))
                for e in range(2, len(entries)):
                    nth = e - first_out
                    if nth == 4:
                        sp.wait_ge(m_ready, 2 * KT)
                        sp.wait_ge(up_done, 4 * KT)
                        sp.dma_start(g_post_row[:, :], g_post.to_broadcast([P, D_MODEL])).then_inc(g_post_loaded, 16)
                    if 4 <= nth < 4 + NQ:
                        n = nth - 4
                        sp.dma_start(x_again[:, n, :], x_v[n]).then_inc(again_loaded[n], 16)
                    load_w(e)
                    kind, j = entries[e - 2]
                    if kind == "kf":
                        if j == 0:
                            sp.wait_ge(neg_c_ready, 1)
                            sp.dma_start(neg_c_dram, neg_c_rows).then_inc(neg_c_stored, 16)
                            sp.wait_ge(neg_c_stored, 16)
                        else:
                            sp.wait_ge(logits_ready, last_score_of_stage[("f", j - 1)].last_piece[1] + 1)
                        for h in range(2):
                            sp.dma_start(neg_c[:, h, :], neg_c_dram[2 * j + h:2 * j + h + 1, :].to_broadcast(
                                [P, LENGTH])).then_inc(neg_c_loaded, 16)

        @block.gpsimd
        def _(pool):
            def split_lo(e):
                s = slot_of(e)
                pool.wait_ge(w_hi_ready, e + 1)
                nc.gpsimd.tensor_tensor(w_low[s], w_raw[s], w_hi[s].bitcast(F32),
                                        ALU.subtract).then_inc(w_ready["pool"], 1)

            for st in steps:
                if st.kind == "split_w" and st.entry < by_pool:
                    split_lo(st.entry)
                if st.kind == "drain" and st.n.last and st.n.name[0] in ("kf", "qf"):
                    kind, j = st.n.name
                    pool.wait_ge(fox_lo_ready, fox_chunks[(kind, j)])
                    for h in range(2):
                        here, there = slice(h * HEAD, (h + 1) * HEAD), slice((1 - h) * HEAD, (2 - h) * HEAD)
                        if kind == "kf":
                            dst, src = kk_f[there, h, :], v_t[here, :].bitcast(F32R)
                        else:
                            dst, src = qq_f[there, h, :], qq_f[here, h, :]
                        pool.dma_start(dst, src).then_inc(fox_stacked[kind], 16)
                if st.kind == "u_square" and st.n in POOL_GAINS:
                    if st.n == POOL_GAINS[0]:
                        pool.wait_ge(g_pre_loaded, 16)
                    pool.wait_ge(x_squared, st.n + 1)
                    nc.gpsimd.tensor_tensor(x_t[st.n], x_t[st.n], g_pre_row[:, :], ALU.mult).then_inc(x_gained, 1)
                if st.kind == "project" and st.name[0] in ("ks", "vs") and st.last:
                    pool.wait_ge(*drained[st.k])
                    keys = st.name[0] == "ks"
                    src = k_s if keys else v_t
                    dst = k_x if keys else v_a_t
                    real = src[:, N_META:].rearrange("p (n w) -> p n w", n=NQ)
                    done = swa_keys_ready if keys else swa_values_ready
                    nc.gpsimd.memset(dst[:, 0, N_META:A_ROWS], 0.0).then_inc(done, 1)
                    nc.gpsimd.tensor_copy(dst[:, 1:, N_META:A_ROWS], real[:, 0:NQ - 1, CHUNK:P]).then_inc(done, 1)
                    for n in range(NQ):
                        nc.gpsimd.tensor_copy(dst[:, n, 0:N_META], src[:, 0:N_META]).then_inc(done, 1)
                    if keys:
                        nc.gpsimd.tensor_copy(dst[:, :, A_ROWS:], real).then_inc(done, 1)
                if st.kind == "finish" and st.n < NQ - 1:
                    n = st.n
                    pool.wait_ge(result_scaled, n + 1)
                    pool.wait_ge(again_loaded[n], 16)
                    nc.gpsimd.tensor_tensor(result[:, n % 2, :], result[:, n % 2, :], x_again[:, n, :],
                                            ALU.add).then_inc(result_ready["pool"], 1)
                if st.kind == "up" and st.b == 1:
                    pool.wait_ge(up_gated, 4 * st.d + 2 * st.c + 2)
                    nc.gpsimd.tensor_tensor(y[:, st.d, st.c * BANK:(st.c + 1) * BANK], gated[:, 0, st.c, :],
                                            gated[:, 1, st.c, :], ALU.add).then_inc(m_ready, 1)

        @block.scalar
        def _(act):
            def split_hi(e):
                s = slot_of(e)
                act.wait_ge(w_loaded[s], w_target[e])
                nc.scalar.activation(w_hi[s], w_raw[s], ACT.Copy).then_inc(w_hi_ready, 1)

            with nc.allow_non_contiguous_dma(reason="a broadcast row"):
                act.dma_start(g_pre_row, g_pre.to_broadcast([P, D_MODEL])).then_inc(g_pre_loaded, 16)
                act.dma_start(ident[:, :], ident_in).then_inc(ident_loaded, 16)

            def store(n):
                who = "pool" if n < NQ - 1 else "dve"
                act.wait_ge(result_ready[who], n + 1 if n < NQ - 1 else 1)
                act.dma_start(out_v[n], result[:, n % 2, :]).then_inc(out_stored[n % 2], 16)

            act.wait_ge(cleared, 1)
            nc.scalar.activation(stat[:, 9, 0:1], stat[:, 9, 1:2], ACT.Sqrt).then_inc(x_rooted, 1)
            for st in steps:
                if st.kind == "split_w":
                    split_hi(st.entry)
                elif st.kind == "u_square":
                    n = st.n
                    r = N_META if n == 0 else P
                    act.wait_ge(x_loaded[n], 16)
                    if n:
                        act.wait_ge(x_squared, n)
                    nc.scalar.activation(squares[0:r, :], x_t[n][0:r, :], ACT.Square,
                                         accum_out=stat[0:r, 0, n:n + 1]).then_inc(x_squared, 1)
                elif st.kind == "u_var":
                    n = st.n
                    act.wait_ge(var_ready, n + 1)
                    nc.scalar.activation(stat[:, 2, n:n + 1], stat[:, 1, n:n + 1], ACT.Sqrt).then_inc(x_rooted, 1)
                elif st.kind == "u_copy":
                    n = st.n
                    r = N_META if n == 0 else P
                    c0 = 0 if n == 0 else N_META + (n - 1) * P
                    for g in range(2 * n, 2 * n + 2):
                        k0 = 4 * (g % 2)
                        act.wait_ge(u_transposed, g + 1)
                        nc.scalar.activation(u_hi[:, k0:k0 + 4, c0:c0 + r], bank4(g % U_RING, r),
                                             ACT.Copy).then_inc(u_hi_ready, 1)
                elif st.kind == "forget":
                    act.wait_ge(f_step, 1)
                    nc.scalar.activation(f_e, f_e, ACT.Exp, scale=-1.0).then_inc(f_back, 1)
                    act.wait_ge(f_back, 1)
                    nc.scalar.activation(f_e, f_e, ACT.Ln, bias=1.0).then_inc(f_back, 1)
                elif st.kind == "project" and st.name[0] in ("zs", "zf"):
                    act.wait_ge(chunk_done, st.k + 1)
                    z_no = z_number[st.k]
                    if z_no:
                        act.wait_ge(z_used, z_no)
                    nc.scalar.activation(z_t[:, 0:st.w], PS[:, PJ_BANK + st.k % 2, 0:st.w], ACT.Tanh,
                                         scale=0.5).then_inc(z_tanh, 1)
                elif st.kind == "project" and st.name[0] in ("kf", "qf"):
                    act.wait_ge(chunk_done, st.k + 1)
                    for h in range(2):
                        part, dst = fox_part(st, h)
                        nc.scalar.activation(dst, PS[part, PJ_BANK + st.k % 2, 0:st.w], ACT.Copy,
                                             scale=SCALE if st.name[0] == "qf" else 1.0).then_inc(fox_hi_ready, 1)
                elif st.kind == "values":
                    for g, who, v, tiles in st.groups:
                        if who == "act":
                            act.wait_ge(transposed, g + 1)
                            dst, src = values_copy(g, tiles)
                            nc.scalar.activation(dst, src, ACT.Copy).then_inc(group_freed["act"], 1)
                elif st.kind == "piece":
                    k, st = st.n.first_piece + st.t, st.n
                    b = st.i % 2
                    for h in range(2):
                        if k != st.last_piece[h]:
                            continue
                        act.wait_ge(logits_ready, k + 1)
                        x_last = max(q[1] for q in st.pieces)
                        width = max(q[2] + q[3] for q in st.pieces)
                        bias = neg_max[:, b, h, x_last:x_last + 1]
                        nc.scalar.activation(probs[:, b, h, 0:width], probs[:, b, h, 0:width], ACT.Exp, bias=bias,
                                             scale=-1.0, accum_out=den[:, b, h:h + 1]).then_inc(exp_done, 1)
                        if st.stage[0] == "s":
                            hh = st.stage[1] + PAIRS * h
                            nc.scalar.activation(es[:, b, h:h + 1], sink[:, hh:hh + 1], ACT.Exp,
                                                 bias=bias).then_inc(exp_done, 1)
                elif st.kind in ("open", "pv"):
                    for g, pg, who, v, tiles in groups_now(st):
                        if who == "act":
                            act.wait_ge(transposed, g + 1)
                            if pg >= PT_RING:
                                act.wait_ge(group_used, pg - PT_RING + 1)
                            nc.scalar.activation(p_t[:, pg % PT_RING, 0:P * len(tiles)],
                                                 PS[:, T_BANK + g % T_RING, 0:P * len(tiles)],
                                                 ACT.Copy).then_inc(group_freed["act"], 1)
                elif st.kind == "split_y":
                    act.wait_ge(group_used, totals["pgroups"])
                    act.wait_ge(z_used, len(z_number))
                    for s in range(2 * PAIRS):
                        nc.scalar.activation(y_hi[:, s, :], y[:, s, :], ACT.Copy).then_inc(y_hi_ready, 1)
                elif st.kind == "gate":
                    k = 4 * st.d + 2 * st.b + st.c
                    act.wait_ge(gate_done, k + 1)
                    if st.d:
                        act.wait_ge(up_gated, 4 * (st.d - 1) + 2 * st.c + st.b + 1)
                    nc.scalar.activation(tanh_g[:, st.b, st.c, :], PS[:, 2 * st.b + st.c, :], ACT.Tanh, scale=0.5,
                                         bias=half_bg[:, st.b, st.d:st.d + 1]).then_inc(gate_tanh, 1)
                elif st.kind == "split_m":
                    if st.k == 0:
                        act.wait_ge(gate_done, 4 * KT)
                    act.wait_ge(m_ready, 2 * st.d + st.c + 1)
                    tok = slice(st.c * BANK, (st.c + 1) * BANK)
                    nc.scalar.activation(m_hi[:, st.d, tok], y[:, st.d, tok], ACT.Copy,
                                         scale=0.5).then_inc(m_hi_ready, 1)
                elif st.kind == "out":
                    act.wait_ge(out_done, st.k + 1)
                    if st.half >= 2:
                        act.wait_ge(natural_done, 2 * OUT_GROUPS[st.half - 1][0])
                    nc.scalar.activation(o_t[:, st.half % 2, st.d, 0:st.w], PS[:, st.k % 4, 0:st.w],
                                         ACT.Copy).then_inc(out_copied, 1)
                elif st.kind == "natural":
                    n, half = st.n, st.half
                    act.wait_ge(natural_done, st.k + 1)
                    if st.k:
                        act.wait_ge(out_squared, st.k)
                    nc.scalar.activation(squares2[:, 0:BANK], natural(n)[:, half * BANK:(half + 1) * BANK], ACT.Square,
                                         accum_out=stat[:, (4, 8)[half], n:n + 1]).then_inc(out_squared, 1)
                elif st.kind == "finish":
                    n = st.n
                    act.wait_ge(out_var, n + 1)
                    nc.scalar.activation(stat[:, 6, n:n + 1], stat[:, 5, n:n + 1], ACT.Sqrt).then_inc(out_rooted, 1)
                    if n:
                        store(n - 1)

            store(NQ - 1)
            act.wait_ge(out_stored[0], 16 * NQ // 2)
            act.wait_ge(out_stored[1], 16 * NQ // 2)

        @block.vector
        def _(dve):
            chain = [0]

            def link(ins):
                chain[0] += 1
                ins.then_inc(dve_chain, 1)
                dve.wait_ge(dve_chain, chain[0])

            def root(base, n):
                b, h, t = (stat[:, base + x, n:n + 1] for x in (1, 2, 3))
                link(nc.vector.reciprocal(t, h))
                link(nc.vector.scalar_tensor_tensor(out=t, in0=t, scalar=b, in1=h, op0=ALU.mult, op1=ALU.add))
                return nc.vector.reciprocal(t, t)

            def norm(st):
                b = st.i % 2
                dve.wait_ge(exp_done, exps_until[st.i + 1])
                if st.stage[0] == "s":
                    link(nc.vector.tensor_tensor(den[:, b, :], den[:, b, :], es[:, b, :], ALU.add))
                link(nc.vector.reciprocal(rec[:, b, :], den[:, b, :]))
                width = max(q[2] + q[3] for q in st.pieces)
                for h in range(2):
                    nc.vector.tensor_scalar(probs[:, b, h, 0:width], probs[:, b, h, 0:width],
                                            rec[:, b, h:h + 1], None, ALU.mult).then_inc(normed, 1)

            nc.vector.memset(stat[:, :, :], 1.0).then_inc(cleared, 1)
            nc.vector.memset(f_ones, 1.0).then_inc(cleared, 1)
            for st in steps:
                if st.kind == "split_w" and st.entry >= by_pool:
                    s = slot_of(st.entry)
                    dve.wait_ge(w_hi_ready, st.entry + 1)
                    nc.vector.tensor_tensor(w_low[s], w_raw[s], w_hi[s].bitcast(F32),
                                            ALU.subtract).then_inc(w_ready["dve"], 1)
                elif st.kind == "u_var":
                    n = st.n
                    dve.wait_ge(x_squared, n + 1)
                    nc.vector.tensor_scalar(stat[:, 1, n:n + 1], stat[:, 0, n:n + 1], 0.25 / D_MODEL, 0.25 * EPS,
                                            ALU.mult, ALU.add).then_inc(var_ready, 1)
                elif st.kind == "u_newton":
                    dve.wait_ge(x_rooted, st.n + 2)
                    root(0, st.n).then_inc(x_newton, 1)
                elif st.kind == "u_norm":
                    n = st.n
                    r = N_META if n == 0 else P
                    if n == 0:
                        dve.wait_ge(g_pre_loaded, 16)
                    dve.wait_ge(x_newton, n + 1)
                    if n in POOL_GAINS:
                        dve.wait_ge(x_gained, POOL_GAINS.index(n) + 1)
                        nc.vector.tensor_scalar(x_t[n], x_t[n], stat[:, 3, n:n + 1], None,
                                                ALU.mult).then_inc(x_normed, 1)
                        continue
                    nc.vector.scalar_tensor_tensor(out=x_t[n][0:r, :], in0=x_t[n][0:r, :],
                                                   scalar=stat[0:r, 3, n:n + 1], in1=g_pre_row[0:r, :], op0=ALU.mult,
                                                   op1=ALU.mult).then_inc(x_normed, 1)
                elif st.kind == "u_lo":
                    n = st.n
                    r = N_META if n == 0 else P
                    c0 = 0 if n == 0 else N_META + (n - 1) * P
                    g = 2 * n + st.t
                    k0 = 4 * st.t
                    dve.wait_ge(u_hi_ready, g + 1)
                    nc.vector.tensor_tensor(u_lo[:, k0:k0 + 4, c0:c0 + r], bank4(g % U_RING, r),
                                            u_hi[:, k0:k0 + 4, c0:c0 + r].bitcast(F32),
                                            ALU.subtract).then_inc(u_ready, 1)
                elif st.kind == "drain":
                    st = st.n
                    kind = st.name[0]
                    src = PS[:, PJ_BANK + st.k % 2, 0:st.w]
                    dve.wait_ge(chunk_done, st.k + 1)
                    if kind == "f":
                        dve.wait_ge(const_loaded, 16 * CONST_LOADS)
                        nc.vector.tensor_scalar(f_x[:, st.t0:st.t0 + st.w], src[0:HEADS, :], bf[:, 0:1], None,
                                                ALU.add).then_inc(chunk_drained, 1)
                    elif kind == "qs":
                        nc.vector.tensor_scalar(q_s[:, st.t0 - N_META:st.t0 - N_META + st.w], src, SCALE, None,
                                                ALU.mult).then_inc(chunk_drained, 1)
                    elif kind == "ks":
                        nc.vector.tensor_copy(k_s[:, st.t0:st.t0 + st.w], src).then_inc(chunk_drained, 1)
                    elif kind in ("qf", "kf"):
                        if kind == "kf" and st.name[1] == 0 and st.c == 0:
                            dve.wait_ge(swa_values_ready, VALUES_COPIES)
                        for h in range(2):
                            part, hi = fox_part(st, h)
                            if kind == "kf":
                                lo = v_t[part, st.t0:st.t0 + st.w].bitcast(F32R)
                            else:
                                lo = q_lo[part, st.t0 - N_META:st.t0 - N_META + st.w]
                            dve.wait_ge(fox_hi_ready, fox_chunk[st.k] * 2 + h + 1)
                            ins = nc.vector.scalar_tensor_tensor(out=lo, in0=src[part, :],
                                                                 scalar=SCALE if kind == "qf" else 1.0,
                                                                 in1=hi.bitcast(F32), op0=ALU.mult, op1=ALU.subtract)
                            ins.then_inc(fox_lo_ready, 1)
                    elif kind in ("vs", "vf"):
                        if kind == "vf" and st.c == 0:
                            dve.wait_ge(fox_stacked["kf"], 32 * (st.name[1] + 1))
                        nc.vector.tensor_copy(v_t[:, st.t0:st.t0 + st.w], src).then_inc(chunk_drained, 1)
                    else:
                        slot = st.name[1] + (0 if kind == "zs" else PAIRS)
                        yy = y[:, slot, st.t0 - N_META:st.t0 - N_META + st.w]
                        zz = z_t[:, 0:st.w]
                        dve.wait_ge(z_tanh, z_number[st.k] + 1)
                        ins = nc.vector.scalar_tensor_tensor(out=zz, in0=zz, scalar=1.0, in1=src, op0=ALU.add,
                                                             op1=ALU.mult)
                        ins.then_inc(chunk_drained, 1)
                        dve.wait_ge(*drained[st.k])
                        nc.vector.scalar_tensor_tensor(out=yy, in0=zz, scalar=0.5, in1=yy, op0=ALU.mult,
                                                       op1=ALU.mult).then_inc(z_used, 1)
                elif st.kind == "forget":
                    nc.vector.tensor_scalar(half_bg[:, :, :], half_bg[:, :, :], 0.5, None, ALU.mult
                                            ).then_inc(cleared, 1)
                    nc.vector.tensor_scalar(neg_sink[:, :], sink[:, :], -1.0, None, ALU.mult).then_inc(cleared, 1)
                    dve.wait_ge(cleared, 4)
                    dve.wait_ge(*drained[2 * len(EARLY_TOKENS) - 2])
                    nc.vector.scalar_tensor_tensor(out=f_e, in0=f_x, scalar=-1.0, in1=f_x, op0=ALU.mult,
                                                   op1=ALU.max).then_inc(f_step, 1)
                    link(nc.vector.tensor_scalar(f_x, f_x, -1.0, 0.0, ALU.mult, ALU.max))
                    dve.wait_ge(f_back, 2)
                    link(nc.vector.tensor_tensor(f_r, f_x, f_e, ALU.add))
                    nc.vector.tensor_tensor_scan(neg_c_rows, f_ones, f_r, 0.0, ALU.mult,
                                                 ALU.add).then_inc(neg_c_ready, 1)
                elif st.kind == "values":
                    for g, who, v, tiles in st.groups:
                        if who == "dve":
                            dve.wait_ge(transposed, g + 1)
                            dst, src = values_copy(g, tiles)
                            nc.vector.tensor_copy(dst, src).then_inc(group_freed["dve"], 1)
                elif st.kind == "piece":
                    y_, st = st.t, st.n
                    b = st.i % 2
                    swa = st.stage[0] == "s"
                    if st.i >= 2 and y_ == 0:
                        dve.wait_ge(transposed, items_done_groups[st.i - 2][0] + 1)
                    if not swa and st.t == 0 and y_ == 0:
                        dve.wait_ge(neg_c_loaded, 32 * (st.stage[1] + 1))
                    h, x_, c0, w = st.pieces[y_]
                    k = st.first_piece + y_
                    hh = st.stage[1] + PAIRS * h
                    dve.wait_ge(scored, k + 1)
                    if x_:
                        dve.wait_ge(logits_ready, k - 1)
                    init = neg_max[:, b, h, x_ - 1:x_] if x_ else (neg_sink[:, hh:hh + 1] if swa else BIG)
                    in1 = alibi[:, hh, :] if swa else neg_c[:, h, c0:c0 + w]
                    nc.vector.tensor_tensor_reduce(probs[:, b, h, c0:c0 + w],
                                                   PS[:, S_BANK + k % S_RING, 0:w], in1, -1.0, init,
                                                   ALU.add, ALU.min,
                                                   neg_max[:, b, h, x_:x_ + 1]).then_inc(logits_ready, 1)
                elif st.kind == "norm":
                    norm(st.n)
                elif st.kind in ("open", "pv"):
                    for g, pg, who, v, tiles in groups_now(st):
                        if who == "dve":
                            dve.wait_ge(transposed, g + 1)
                            if pg >= PT_RING:
                                dve.wait_ge(group_used, pg - PT_RING + 1)
                            nc.vector.tensor_copy(p_t[:, pg % PT_RING, 0:P * len(tiles)],
                                                  PS[:, T_BANK + g % T_RING, 0:P * len(tiles)]
                                                  ).then_inc(group_freed["dve"], 1)
                elif st.kind == "y_copy":
                    dve.wait_ge(group_used, st.groups[-1][1] + 1)
                    slot = st.stage[1] + (0 if st.stage[0] == "s" else PAIRS)
                    nc.vector.tensor_copy(y[:, slot, st.t * P:(st.t + 1) * P],
                                          PS[:, Y_BANK, 0:P]).then_inc(y_copied, 1)
                elif st.kind == "split_y":
                    for s in range(2 * PAIRS):
                        dve.wait_ge(y_hi_ready, s + 1)
                        nc.vector.tensor_tensor(y_lo[:, s, :], y[:, s, :], y_hi[:, s, :].bitcast(F32),
                                                ALU.subtract).then_inc(y_split, 1)
                elif st.kind == "up":
                    dve.wait_ge(up_done, 4 * st.d + 2 * st.c + st.b + 1)
                    dve.wait_ge(gate_tanh, 4 * st.d + 2 * st.b + st.c + 1)
                    if st.d:
                        dve.wait_ge(m_ready, 2 * (st.d - 1) + st.c + 1)
                    nc.vector.scalar_tensor_tensor(out=gated[:, st.b, st.c, :], in0=tanh_g[:, st.b, st.c, :],
                                                   scalar=1.0, in1=PS[:, 4 + 2 * st.b + st.c, :], op0=ALU.add,
                                                   op1=ALU.mult).then_inc(up_gated, 1)
                elif st.kind == "split_m":
                    dve.wait_ge(m_hi_ready, st.k + 1)
                    tok = slice(st.c * BANK, (st.c + 1) * BANK)
                    nc.vector.scalar_tensor_tensor(out=m_lo[:, st.d, tok], in0=y[:, st.d, tok], scalar=0.5,
                                                   in1=m_hi[:, st.d, tok].bitcast(F32), op0=ALU.mult,
                                                   op1=ALU.subtract).then_inc(m_split, 1)
                elif st.kind == "natural":
                    n = st.n
                    dve.wait_ge(out_squared, st.k + 1)
                    if st.half == 0:
                        link(nc.vector.tensor_scalar(stat[:, 9, n:n + 1], stat[:, 4, n:n + 1], 0.25 / D_MODEL,
                                                     0.25 * EPS, ALU.mult, ALU.add))
                    else:
                        nc.vector.scalar_tensor_tensor(out=stat[:, 5, n:n + 1], in0=stat[:, 8, n:n + 1],
                                                       scalar=0.25 / D_MODEL, in1=stat[:, 9, n:n + 1], op0=ALU.mult,
                                                       op1=ALU.add).then_inc(out_var, 1)
                elif st.kind == "finish":
                    n = st.n
                    dve.wait_ge(out_rooted, n + 1)
                    link(root(4, n))
                    if n == 0:
                        dve.wait_ge(g_post_loaded, 16)
                    if n >= 2:
                        dve.wait_ge(out_stored[n % 2], 16 * (n // 2))
                    nc.vector.scalar_tensor_tensor(out=result[:, n % 2, :], in0=natural(n),
                                                   scalar=stat[:, 7, n:n + 1], in1=g_post_row[:, :], op0=ALU.mult,
                                                   op1=ALU.mult).then_inc(result_scaled, 1)
                    if n == NQ - 1:
                        dve.wait_ge(result_scaled, n + 1)
                        dve.wait_ge(again_loaded[n], 16)
                        nc.vector.tensor_tensor(result[:, n % 2, :], result[:, n % 2, :], x_again[:, n, :],
                                                ALU.add).then_inc(result_ready["dve"], 1)

        @block.tensor
        def _(pe):
            def three(dst, e, k, hi, lo, first, last):
                s = slot_of(e)
                pe.matmul(dst, w_hi[s][:, k, :], hi, start=first, stop=False)
                pe.matmul(dst, w_hi[s][:, k, :], lo, start=False, stop=False)
                return pe.matmul(dst, w_low[s][:, k, :], hi, start=False, stop=last)

            def free_bank_of(g):
                if g >= T_RING:
                    who, v = owner[g - T_RING]
                    pe.wait_ge(group_freed[who], v)

            pe.wait_ge(ident_loaded, 16)
            for st in steps:
                if st.kind in ("project", "gate", "up", "out"):
                    pe.wait_ge(*split_done(st.entry))
                if st.kind == "u_norm":
                    n = st.n
                    r = N_META if n == 0 else P
                    pe.wait_ge(x_normed, n + 1)
                    for g in range(2 * n, 2 * n + 2):
                        if g >= U_RING:
                            pe.wait_ge(u_ready, g - U_RING + 1)
                        for j in range(4):
                            k = 4 * (g % 2) + j
                            ins = pe.transpose(PS[:, g % U_RING, j * P:j * P + r],
                                               x_t[n][0:r, k * P:(k + 1) * P], ident[0:r, 0:r])
                        ins.then_inc(u_transposed, 1)
                elif st.kind == "project":
                    tiles = -(-(st.t0 + st.w - N_META) // P) + 1
                    pe.wait_ge(u_ready, 2 * tiles)
                    if st.k >= 2:
                        pe.wait_ge(*drained[st.k - 2])
                    dst = PS[:, PJ_BANK + st.k % 2, 0:st.w]
                    tok = slice(st.t0, st.t0 + st.w)
                    for k in range(KT):
                        ins = three(dst, st.entry, k, u_hi[:, k, tok], u_lo[:, k, tok], k == 0, k == KT - 1)
                    ins.then_inc(chunk_done, 1)
                elif st.kind == "values":
                    swa = st.name[0] == "vs"
                    pe.wait_ge(*drained[values_chunk[st.name]])
                    if swa:
                        pe.wait_ge(swa_values_ready, VALUES_COPIES)
                    for g, who, v, tiles in st.groups:
                        free_bank_of(g)
                        for j, (what, n) in enumerate(tiles):
                            if what == "a":
                                src, r = v_a_t[:, n, :], A_ROWS
                            elif what == "b" or n:
                                m = n if what == "b" else n - 1
                                src, r = v_t[:, N_META + m * P:N_META + (m + 1) * P], P
                            else:
                                src, r = v_t[:, 0:P], P
                            ins = pe.transpose(PS[0:r, T_BANK + g % T_RING, j * P:(j + 1) * P], src, ident[:, :])
                        ins.then_inc(transposed, 1)
                elif st.kind == "piece":
                    y_, st = st.t, st.n
                    swa = st.stage[0] == "s"
                    if y_ == 0:
                        if swa:
                            pe.wait_ge(*drained[q_chunk[st.stage]])
                            pe.wait_ge(swa_keys_ready, KEYS_COPIES)
                        else:
                            for kind in ("kf", "qf"):
                                pe.wait_ge(fox_stacked[kind], 32 * (st.stage[1] + 1))
                    if st.i == 0:
                        pe.wait_ge(u_ready, 2 * (NQ + 1))
                    h, x_, c0, w = st.pieces[y_]
                    k = st.first_piece + y_
                    hh = st.stage[1] + PAIRS * h
                    if k >= S_RING:
                        pe.wait_ge(logits_ready, k - S_RING + 1)
                    bank = PS[:, S_BANK + k % S_RING, :]
                    rows_ = slice(h * HEAD, (h + 1) * HEAD)
                    more = swa or c0 + w == N_META + (st.t + 1) * P
                    tok = slice(st.t * P, (st.t + 1) * P)
                    if swa:
                        ins = pe.matmul(bank[:, 0:w], q_s[rows_, tok], k_x[rows_, st.t, :], start=True, stop=False)
                    else:
                        pe.matmul(bank[:, 0:w], qq_f[:, h, tok], kk_f[:, h, c0:c0 + w], start=True, stop=False)
                        ins = pe.matmul(bank[:, 0:w], q_lo[rows_, tok], kk_f[rows_, h, c0:c0 + w], start=False,
                                        stop=not more)
                    if swa and st.t == 0:
                        ins = pe.matmul(bank[:, 0:A_ROWS], ones_row, first_block_row, start=False, stop=True)
                    elif swa:
                        ins = pe.matmul(bank[:, 0:N_META], ones_row,
                                        meta_far_row[:, hh, st.t:st.t + 1].to_broadcast([1, N_META]), start=False,
                                        stop=True)
                    elif more:
                        ins = pe.matmul(bank[:, w - P:w], ident_b, causal, start=False, stop=True)
                    ins.then_inc(scored, 1)
                elif st.kind in ("open", "pv"):
                    number_, st = st.t, st.n if st.kind == "pv" else st
                    opening = st.kind == "open"
                    b = st.i % 2
                    swa = st.stage[0] == "s"

                    def transposes(n):
                        g, pg, who, v, tiles = st.groups[n]
                        free_bank_of(g)
                        for j, (h, x_, c0, w) in enumerate(tiles):
                            pe.wait_ge(normed, 2 * st.i + h + 1)
                            w = P if w == N_META else w
                            ins = pe.transpose(PS[0:w, T_BANK + g % T_RING, j * P:(j + 1) * P],
                                               probs[:, b, h, c0:c0 + w], ident[:, :])
                        ins.then_inc(transposed, 1)

                    def values(n):
                        g, pg, who, v, tiles = st.groups[n]
                        pe.wait_ge(group_freed[who], v)
                        for j, (h, x_, c0, w) in enumerate(tiles):
                            cols = slice(h * HEAD, (h + 1) * HEAD)
                            vv = (v_a, v_b)[x_][0:w, st.t, cols] if swa else v_f[0:w, x_, cols]
                            ins = pe.matmul(PS[h * HEAD:(h + 1) * HEAD, Y_BANK, 0:P], vv,
                                            p_t[0:w, pg % PT_RING, j * P:(j + 1) * P], start=x_ == 0,
                                            stop=x_ == st.n_tiles - 1)
                        ins.then_inc(group_used, 1)

                    if opening:
                        for n in range(len(st.groups[:2])):
                            transposes(n)
                        continue
                    n = number_
                    if n == 0 and st.i:
                        pe.wait_ge(y_copied, st.i)
                    if n == 0 and st.t == 0:
                        for w_, v_ in values_ready[("s", 0) if swa else st.stage].items():
                            pe.wait_ge(group_freed[w_], v_)
                    values(n)
                    if n + 2 < len(st.groups):
                        transposes(n + 2)
                elif st.kind == "gate":
                    if st.d == 0 and st.b == 0 and st.c == 0:
                        pe.wait_ge(*drained[totals["chunks"] - 1])
                        pe.wait_ge(y_copied, totals["items"])
                    if st.d:
                        pe.wait_ge(gate_tanh, 4 * (st.d - 1) + 2 * st.b + st.c + 1)
                    tok = slice(N_META + st.c * BANK, N_META + (st.c + 1) * BANK)
                    for k in range(KT):
                        ins = three(PS[:, 2 * st.b + st.c, :], st.entry, k, u_hi[:, k, tok], u_lo[:, k, tok],
                                    k == 0, k == KT - 1)
                    ins.then_inc(gate_done, 1)
                elif st.kind == "up":
                    if st.d == 0:
                        pe.wait_ge(y_split, PAIRS * (st.b + 1))
                    if st.d:
                        pe.wait_ge(up_gated, 4 * (st.d - 1) + 2 * st.c + st.b + 1)
                    tok = slice(st.c * BANK, (st.c + 1) * BANK)
                    for j in range(PAIRS):
                        k = PAIRS * st.b + j
                        ins = three(PS[:, 4 + 2 * st.b + st.c, :], st.entry, k, y_hi[:, k, tok], y_lo[:, k, tok],
                                    j == 0, j == PAIRS - 1)
                    ins.then_inc(up_done, 1)
                elif st.kind == "out":
                    if st.k == 0:
                        pe.wait_ge(gate_tanh, 4 * KT)
                    if st.k == KT:
                        pe.wait_ge(m_split, 2 * KT)
                    if st.k >= 4:
                        pe.wait_ge(out_copied, st.k - 3)
                    tok = slice(st.t0, st.t0 + st.w)
                    for k in range(KT):
                        if st.k == 0:
                            pe.wait_ge(m_split, k + 1)
                        ins = three(PS[:, st.k % 4, 0:st.w], st.entry, k, m_hi[:, k, tok], m_lo[:, k, tok], k == 0,
                                    k == KT - 1)
                    ins.then_inc(out_done, 1)
                elif st.kind == "natural":
                    n = st.n
                    g = sum(1 for n0, _ in OUT_GROUPS if n0 <= n) - 1
                    if st.k == 0:
                        pe.wait_ge(up_gated, 4 * KT)
                    pe.wait_ge(out_copied, KT * g + 4 * (st.half + 1))
                    if n >= 2:
                        pe.wait_ge(result_scaled, n - 1)
                    t = n - OUT_GROUPS[g][0]
                    for d in range(4 * st.half, 4 * st.half + 4):
                        ins = pe.transpose(PS[:, 4 + 2 * (n % 2) + d // 4, (d % 4) * P:(d % 4 + 1) * P],
                                           o_t[:, g % 2, d, t * P:(t + 1) * P], ident[:, :])
                    ins.then_inc(natural_done, 1)


_INS = ["x", "meta_tokens", "g_pre", "w_in", "b_forget", "b_gate", "sinks", "w_up_swa", "w_up_fox", "w_out",
        "g_post"]


def constants():
    def bf16_bits(a):
        return (np.ascontiguousarray(a, np.float32).view(np.uint32) >> 16).astype(np.uint16)

    slopes = 2.0 ** -np.arange(1, HEADS + 1)
    ident = np.eye(P, dtype=np.float32)
    a, c = np.arange(P)[:, None], np.arange(P)[None, :]
    causal = np.where(c <= a, 0.0, MASK)
    meta = N_META + a - np.arange(N_META)[None, :]
    back = a - (np.arange(CHUNK)[None, :] - CHUNK)
    dist = np.concatenate([meta, back, np.abs(a - c)], axis=1)
    ok = np.concatenate([np.ones((P, N_META), bool), np.broadcast_to(a < CHUNK, (P, CHUNK)),
                         (c // CHUNK) <= (a // CHUNK)], axis=1)
    alibi = np.where(ok[:, None, :], -slopes[None, :, None] * dist[:, None, :], MASK)
    const = bf16_bits(np.concatenate([ident, causal, alibi.reshape(P, -1)], axis=1))
    first = np.where(np.arange(A_ROWS) < N_META, 0.0, MASK)
    far = -slopes[:, None] * P * np.arange(NQ)[None, :]
    rows = bf16_bits(np.concatenate([np.ones(P), first, far.reshape(-1)])[None, :])
    return {"ident": ident, "const": const, "rows": rows}


def kernel(**inputs):
    import concourse.bacc as _bacc
    from concourse.bass_utils import run_bass_kernel_spmd as _run

    nc = _bacc.Bacc("TRN2", target_bir_lowering=False, num_devices=1)
    arrays, args = {}, []
    data = {n: np.ascontiguousarray(inputs[n]) for n in _INS}
    data.update(constants())
    for name, a in data.items():
        arrays[f"in_{name}_dram"] = a
        args.append(nc.dram_tensor(f"in_{name}_dram", a.shape, mybir.dt.from_np(a.dtype), kind="ExternalInput").ap())
    args.append(nc.dram_tensor("out_dram", (1, SEQ, D_MODEL), F32, kind="ExternalOutput").ap())
    build(nc, *args)
    return _run(nc, [arrays], core_ids=[0]).results[0]["out_dram"]
```

```python
from contextlib import ExitStack

import numpy as np

import concourse.bass as bass
from concourse import mybir

F32 = mybir.dt.float32
F32R = mybir.dt.float32r
BF16 = mybir.dt.bfloat16
ALU = mybir.AluOpType
ACT = mybir.ActivationFunctionType

P = 128
D_MODEL = 1024
SEQ = 1024
N_META = 16
LENGTH = SEQ + N_META
HEAD = 64
HEADS = 8
CHUNK = 64
KT = D_MODEL // P
NQ = SEQ // P
BANK = 512
EPS = 1e-6
SCALE = HEAD ** -0.5
MASK = -1e30
BIG = 3e38
PAIRS = 4
W_SWA = N_META + CHUNK + P
W_SLOTS = 10
F_LOW = 32
A_ROWS = N_META + CHUNK

COL_QA, COL_KA, COL_VA, COL_ZA = 0, 512, 640, 768
COL_QF, COL_KF, COL_VF, COL_ZF = 1280, 1792, 2304, 2816
COL_FF, COL_GA, COL_GF = 3328, 3336, 4360

ALL_TOKENS = [(0, 352), (352, 352), (704, 336)]
EARLY_TOKENS = [(0, N_META + 2 * P)] + [(N_META + 2 * P * x, 2 * P) for x in range(1, 4)]
REAL_TOKENS = [(N_META + 2 * P * x, 2 * P) for x in range(4)]

OUT_GROUPS = [(0, 4), (4, 2), (6, 2)]

U_RING = 4
EARLY_CHUNKS = 12

FILL = {("s", 11): (2, 1, 1, 1, 1, 1, 2, 2), ("s", 8): (1,) * NQ,
        ("f", 12): (2, 2, 1, 1, 2, 1, 2, 1), ("f", 8): (1,) * NQ}
POOL_GAINS = (3, 4, 6, 7, 8)
S_RING = 3
T_RING = 2
PT_RING = 3
AGAIN_RING = 3

BOTH = 2

COPY_ENGINE = ("act", "act", "dve", "act", "dve")


class Step:

    def __init__(self, kind, name=None, entry=None, c=None, t0=None, w=None, last=None, n=None, i=None, b=None,
                 d=None, half=None, t=None, k=None):
        self.kind = kind
        self.name = name
        self.entry = entry
        self.c = c
        self.t0 = t0
        self.w = w
        self.last = last
        self.n = n
        self.i = i
        self.b = b
        self.d = d
        self.half = half
        self.t = t
        self.k = k
        self.stage = None
        self.groups = []
        self.pieces = []
        self.first_piece = None
        self.last_piece = None
        self.n_tiles = None


def entries_of():
    out = [("f", 0), ("ks", 0), ("qs", 0), ("vs", 0)]
    for j in range(PAIRS):
        out += [("kf", j), ("qf", j), ("vf", j)]
        out += ([("qs", j + 1)] if j + 1 < PAIRS else []) + [("zs", j)] + ([("zf", j - 1)] if j else [])
    out += [("zf", PAIRS - 1)]
    for d in range(KT):
        out += [("ga", d), ("gf", d), ("up", d)]
    out += [("out", d) for d in range(KT)]
    return out


def item_of(stage, t):
    if stage[0] == "s":
        tiles = [(0, A_ROWS), (A_ROWS, P)]
        pieces = [(0, W_SWA)]
    else:
        tiles = [(0, N_META)] + [(N_META + P * j, P) for j in range(t + 1)]
        n = t + 1
        k = -(-(N_META + P * n) // BANK)
        per = [n // k + (1 if x < n % k else 0) for x in range(k)]
        per.sort()
        pieces, at = [], 0
        for x, c in enumerate(per):
            w = P * c + (N_META if x == 0 else 0)
            pieces.append((at, w))
            at += w
    return tiles, pieces


def schedule():
    entries = entries_of()
    number = {}
    for e, name in enumerate(entries):
        number.setdefault(name, []).append(e)
    steps = []

    def project(name):
        out = []
        early = name[0] in ("f", "ks")
        ranges = EARLY_TOKENS if early else ALL_TOKENS if name[0] in ("vs", "kf", "vf") else REAL_TOKENS
        for c, (t0, w) in enumerate(ranges):
            out.append(Step("project", name=name, entry=number[name][0], c=c, t0=t0, w=w,
                            last=c == len(ranges) - 1))
            if not early:
                out.append(Step("drain", n=out[-1]))
        if name[0] in ("vs", "vf"):
            out.append(Step("values", name=name))
        return out

    chains = [project((kind, 0)) for kind in ("f", "ks", "qs")]
    early = {m: [] for m in range(NQ + 4)}
    for c in range(4):
        for x in range(3):
            early[4 + 2 * c + (x + 1) // 2].append(chains[x][2 * c if x == 2 else c])
    steps.append(Step("u_square", n=0))
    for m in range(NQ + 4):
        tile = m <= NQ
        if tile:
            steps.append(Step("u_var", n=m))
        if m + 1 <= NQ:
            steps.append(Step("u_square", n=m + 1))
        if 1 <= m <= NQ + 1:
            steps.append(Step("u_copy", n=m - 1))
        subs = [Step("u_lo", n=m - 2, t=g) for g in range(2)] if 2 <= m <= NQ + 2 else []
        steps += subs[:2 if m == 4 else 1]
        if tile:
            steps.append(Step("u_newton", n=m))
        steps += subs[2 if m == 4 else 1:]
        steps += early[m]
        if tile:
            steps.append(Step("u_norm", n=m))
        if m:
            steps += [Step("drain", n=x) for x in early[m - 1]]
        steps += [Step("split_w", entry=e) for e, turn in enumerate((1, 3, 4, 9)) if turn == m]
    steps += [Step("drain", n=x) for x in early[NQ + 3]]
    values_s, keys_f = project(("vs", 0)), project(("kf", 0))
    steps += [Step("split_w", entry=4), Step("place_keys", t=0), Step("place_keys", t=1)]
    steps += values_s[:2] + [Step("forget", t=0)] + values_s[2:-1] + [Step("forget", t=1)]
    steps += keys_f[:4] + values_s[-1:]
    stages = [(b, j) for j in range(PAIRS) for b in ("s", "f")]
    items = [(st, t) for st in stages for t in range(NQ)]
    head = Step("score", i=0)
    steps += [head, Step("piece", n=head), keys_f[4], Step("norm", n=head), keys_f[5]]
    for s, (b, j) in enumerate(stages):
        fill = []
        if b == "s":
            names = [("kf", j), ("qf", j), ("vf", j)]
        else:
            names = ([("qs", j + 1)] if j + 1 < PAIRS else []) + [("zs", j)] + ([("zf", j - 1)] if j else [])
        for name in names:
            for x in project(name) if name != ("kf", 0) else []:
                if x.kind == "drain":
                    fill[-1].append(x)
                else:
                    fill.append([x])
        if s == 0:
            fill[1].insert(0, fill[0].pop())
        for t in range(NQ):
            i = s * NQ + t
            attend = Step("open", i=i)
            steps.append(attend)
            if i + 1 < len(items):
                following = Step("score", i=i + 1)
                steps += [following, Step("piece", n=following)]
            else:
                following = None
            steps.append(Step("close", i=i, n=attend))
            if following:
                steps.append(Step("norm", n=following))
            fills = FILL[(b, len(fill))]
            units = fill[sum(fills[:t]):sum(fills[:t + 1])]
            if units:
                steps += units[0]
            steps += [Step("last_pv", i=i, n=attend), Step("y_copy", i=i, n=attend)]
            for unit in units[1:]:
                steps += unit
    steps += project(("zf", PAIRS - 1))
    for d in range(KT):
        for b, g in enumerate(("ga", "gf")):
            for c in range(2):
                steps.append(Step("gate", b=b, d=d, c=c, entry=number[(g, d)][0], last=c == 1))
                if d == 0 and b == 0 and c == 0:
                    steps.append(Step("split_y"))
        ups = [[Step("up", b=b, d=d, c=c, entry=number[("up", d)][0], last=b == 1 and c == 1) for b in range(2)]
               for c in range(2)]
        if d < KT - 1:
            steps += ups[0] + ups[1]
        else:
            splits = [[Step("split_m", d=x, c=c, k=KT * c + x) for x in range(KT)] for c in range(2)]
            steps += splits[0][:3] + ups[0] + splits[0][3:] + ups[1]
    for g, (n0, n) in enumerate(OUT_GROUPS):
        for d in range(KT):
            steps.append(Step("out", half=g, d=d, t0=n0 * P, w=n * P, entry=number[("out", d)][0], last=True,
                              k=KT * g + d))
            if g == 0 and d == 0:
                steps += splits[1]
            if g and d % 2 and d // 2 < OUT_GROUPS[g - 1][1]:
                steps += [Step("natural", n=OUT_GROUPS[g - 1][0] + d // 2, half=part) for part in range(2)]
            if g and d % 2 == 0 and 1 <= d // 2 <= OUT_GROUPS[g - 1][1]:
                steps += [Step(kind, n=OUT_GROUPS[g - 1][0] + d // 2 - 1) for kind in ("root", "finish")]
            if g == 2 and d == 0:
                steps += [Step("root", n=3), Step("finish", n=3)]
            if g == len(OUT_GROUPS) - 1 and d == KT - 2:
                steps += [Step("natural", n=x, half=0) for x in range(n0, n0 + n)]
    steps += [Step("natural", n=x, half=1) for x in range(n0, n0 + n)] + [
        Step(kind, n=x) for kind in ("root", "finish") for x in range(n0, n0 + n)]

    timed, seen = [], 5
    for st in steps:
        if st.entry is not None and st.kind != "split_w" and st.entry > 2:
            while seen < len(entries) and seen <= st.entry + (2 if st.kind == "out" else 1):
                timed.append(Step("split_w", entry=seen))
                seen += 1
        timed.append(st)
    steps = timed

    n_piece = n_group = n_pgroup = n_chunk = n_natural = 0
    freed = {"act": 0, "dve": 0}
    for st in steps:
        if st.kind == "project":
            st.k = n_chunk
            n_chunk += 1
        elif st.kind == "natural":
            st.k = n_natural
            n_natural += 1
        elif st.kind == "values":
            if st.name[0] == "vf":
                tiles = [("f", x) for x in range(NQ + 1)]
                cut = [tiles[1:5], tiles[5:9], tiles[0:1]]
            else:
                a, b = [("a", x) for x in range(NQ)], [("b", x) for x in range(NQ)]
                cut = [a[0:4], a[4:8], b[0:4], b[4:8]]
            st.groups = []
            for tiles in cut:
                who = ("act", "dve")[n_group % 2]
                freed[who] += 1
                st.groups.append((n_group, who, freed[who], tiles))
                n_group += 1
        elif st.kind in ("close", "last_pv", "y_copy"):
            st.stage, st.t, st.groups, st.n_tiles = st.n.stage, st.n.t, st.n.groups, st.n.n_tiles
        elif st.kind == "score":
            st.stage, st.t = items[st.i]
            _, pieces = item_of(st.stage, st.t)
            st.pieces = [(h, x, c0, w) for x, (c0, w) in enumerate(pieces) for h in range(2)]
            st.first_piece = n_piece
            n_piece += len(st.pieces)
            st.last_piece = {h: max(n_piece - len(st.pieces) + y for y, q in enumerate(st.pieces) if q[0] == h)
                             for h in range(2)}
        elif st.kind == "open":
            st.stage, st.t = items[st.i]
            tiles, _ = item_of(st.stage, st.t)
            every = [(h, x, c0, w) for x, (c0, w) in enumerate(tiles) for h in range(2)]
            if st.stage[0] == "f":
                every = [(BOTH, 0, 0, P)] + every[2:]
            st.n_tiles = len(tiles)
            st.groups = []
            for a in range(0, len(every), 4):
                who = COPY_ENGINE[a // 4]
                freed[who] += 1
                st.groups.append((n_group, n_pgroup, who, freed[who], every[a:a + 4]))
                n_group += 1
                n_pgroup += 1
    owner = {}
    for st in steps:
        for g in groups_of(st):
            owner[g[0]] = (g[-3], g[-2])
    totals = dict(pieces=n_piece, groups=n_group, pgroups=n_pgroup, chunks=n_chunk,
                  freed=dict(freed), items=len(items))
    woven, waiting = [], []
    for st in steps:
        if st.kind == "piece":
            score = st.n
            pieces = [Step("piece", i=score.i, n=score, t=y) for y in range(len(score.pieces))]
            now = len(pieces) if score.i == 0 else S_RING
            woven += pieces[:now]
            waiting = pieces[now:]
        elif st.kind == "close":
            for g in range(len(st.groups) - 1):
                woven.append(Step("pv", i=st.i, n=st, t=g))
                woven += waiting[:1]
                waiting = waiting[1:]
            woven += waiting
            waiting = []
        elif st.kind == "last_pv":
            woven.append(Step("pv", i=st.i, n=st, t=len(st.groups) - 1))
        elif st.kind != "score":
            woven.append(st)
    steps = woven
    return entries, steps, owner, totals


def groups_of(st):
    return st.groups if st.kind in ("values", "open") else []


def build(nc, x, meta_tokens, g_pre, w_in, b_forget, b_gate, sinks, w_up_swa, w_up_fox, w_out, g_post,
          ident_in, const_in, rows_in, out):
    entries, steps, owner, totals = schedule()
    items_done_groups = {}
    for st in steps:
        if st.kind == "open":
            items_done_groups[st.i] = st.groups[-1]

    x_v = x.rearrange("b (n p) d -> (b n) p d", p=P)
    out_v = out.rearrange("b (n p) d -> (b n) p d", p=P)
    w_v = w_in.rearrange("o (k p) c -> p (o k) c", p=P)
    wo_v = w_out.rearrange("o (k p) c -> p (o k) c", p=P)
    wuf_v = w_up_fox.rearrange("o (k p) c -> p (o k) c", p=P)
    wus_v = w_up_swa.rearrange("o (g k p) c -> (o g) p k c", g=2, p=HEAD)
    neg_c_dram = nc.dram_tensor("neg_c_dram", (HEADS, LENGTH), F32).ap()

    with ExitStack() as ctx:
        def sb(name, shape, dt=F32, on=ctx):
            return on.enter_context(nc.sbuf_tensor(name, shape, dt))

        def sem(name):
            return ctx.enter_context(nc.semaphore(name))

        PS = ctx.enter_context(nc.psum_tensor("PS", [P, 8, BANK], F32))
        S_BANK, T_BANK, Y_BANK, PJ_BANK = 0, 3, 5, 6

        once = ExitStack()
        u_hi = sb("u_hi", [P, KT, LENGTH], F32R)
        u_lo = sb("u_lo", [P, KT, LENGTH], F32R)
        y = sb("y", [P, 2 * PAIRS, SEQ], on=once)
        w_raw_slots = sb("w_raw_slots", [P, 2, KT, P], on=once)
        once.close()
        y_r = sb("y_r", [P, 2 * PAIRS, SEQ], F32R)
        w_low_slots = sb("w_low_slots", [P, 2, KT, P], F32R)
        w_hi_slots = sb("w_hi_slots", [P, 2, KT, P], F32R)
        ident = sb("ident", [P, P])
        half_bg = sb("half_bg", [P, 2, KT])
        stat = sb("stat", [P, 10, NQ + 1])

        att = ExitStack()
        const = sb("const", [P, 2 * P + HEADS * W_SWA], BF16, on=att)
        rows = sb("rows", [1, P + A_ROWS + HEADS * NQ], BF16, on=att)
        sink = sb("sink", [P, HEADS], on=att)
        neg_sink = sb("neg_sink", [P, HEADS], on=att)
        bf = sb("bf", [HEADS, 1], on=att)
        qq_s = sb("qq_s", [P, 2, SEQ], F32R, on=att)
        first, second = ExitStack(), ExitStack()
        w_raw_third = sb("w_raw_third", [P, KT, P], on=first)
        first.close()
        qq_f = sb("qq_f", [P, 2, SEQ], F32R, on=att)
        q_lo = sb("q_lo", [P, SEQ], F32R, on=att)
        w_raw_fourth = sb("w_raw_fourth", [P, KT, P], on=second)
        second.close()
        kk_f = sb("kk_f", [P, 2, LENGTH], F32R, on=att)
        v_t = sb("v_t", [P, LENGTH], on=att)
        kk_s = sb("kk_s", [P, 2, NQ, W_SWA], F32R, on=att)
        v_a = sb("v_a", [P, NQ, P], on=att)
        v_b = sb("v_b", [P, NQ, P], on=att)
        v_f = sb("v_f", [P, NQ + 1, P], on=att)
        neg_c = sb("neg_c", [P, 2, LENGTH], on=att)
        probs_ring = [sb("probs_even", [P, 2, LENGTH - P], on=att), sb("probs_odd", [P, 2, LENGTH], on=att)]
        meta_probs = sb("meta_probs", [P, 2, P], on=att)
        p_t = sb("p_t", [P, PT_RING, BANK], on=att)
        z_t = sb("z_t", [P, 2 * P], on=att)
        neg_max = sb("neg_max", [P, 2, 2, 3], on=att)
        den = sb("den", [P, 2, 2], on=att)
        es = sb("es", [P, 2, 2], on=att)
        rec = sb("rec", [P, 2, 2], on=att)
        att.close()
        mrg = ExitStack()
        y_hi = sb("y_hi", [P, 2 * PAIRS, SEQ], F32R, on=mrg)
        y_lo = sb("y_lo", [P, 2 * PAIRS, SEQ], F32R, on=mrg)
        tanh_g = sb("tanh_g", [P, 2, 2, BANK], on=mrg)
        gated = sb("gated", [P, 2, 2, BANK], on=mrg)
        mrg.close()
        fin = ExitStack()
        o_t = sb("o_t", [P, 2, KT, BANK], on=fin)
        g_post_row = sb("g_post_row", [P, D_MODEL], on=fin)
        x_again = sb("x_again", [P, AGAIN_RING, D_MODEL], on=fin)
        result = sb("result", [P, 2, D_MODEL], on=fin)
        squares2 = sb("squares2", [P, BANK], on=fin)
        w_hi_late = sb("w_hi_late", [P, 2, KT, P], F32R, on=fin)
        late = ExitStack()
        w_raw_late = sb("w_raw_late", [P, 2, KT, P], on=late)
        late.close()
        w_low_late = sb("w_low_late", [P, 2, KT, P], F32R, on=fin)
        fin.close()

        ident_b = const[:, 0:P]
        causal = const[:, P:2 * P]
        alibi = const[:, 2 * P:].rearrange("p (h w) -> p h w", h=HEADS)
        ones_row = rows[0:1, 0:P]
        first_block_row = rows[0:1, P:P + A_ROWS]
        meta_far_row = rows[0:1, P + A_ROWS:].rearrange("o (h n) -> o h n", h=HEADS)

        x_t = [v_a[:, :, :].rearrange("p a b -> p (a b)")] + [y[:, i, :] for i in range(NQ - 1)]
        x_t.append(p_t[:, 0:2, :].rearrange("p a b -> p (a b)"))
        squares = probs_ring[1][:, :, :].rearrange("p a b -> p (a b)")[:, 0:D_MODEL]
        g_pre_row = v_b[:, :, :].rearrange("p a b -> p (a b)")
        q_lo_s = y_r[:, 2 * PAIRS - 1, :]
        k_s_hi, k_s_lo = (y_r[:, x:x + 2, :].rearrange("p a b -> p (a b)")[:, 0:LENGTH] for x in (0, 2))
        neg_c_rows = y[0:HEADS, 5:7, :].rearrange("p a b -> p (a b)")[:, 0:LENGTH]
        v_a_t = y[:, PAIRS, 0:NQ * A_ROWS].rearrange("p (n w) -> p n w", n=NQ)
        f_x = neg_c[0:HEADS, 0, :]
        f_e = neg_c[0:HEADS, 1, :]
        f_ones = probs_ring[0][0:HEADS, :, :].rearrange("p a b -> p (a b)")[:, 0:LENGTH]
        m_hi, m_lo = u_hi, u_lo
        w_raw = [w_raw_slots[:, 0], w_raw_slots[:, 1], w_raw_third[:, :, :], w_raw_fourth[:, :, :]]
        w_low = [w_low_slots[:, 0], w_low_slots[:, 1]] + [x[:, 0, 0:D_MODEL].rearrange("p (k c) -> p k c", k=KT)
                                                          for x in (qq_f, kk_f)]
        w_hi = [w_hi_slots[:, 0], w_hi_slots[:, 1]] + [x[:, 1, 0:D_MODEL].rearrange("p (k c) -> p k c", k=KT)
                                                       for x in (qq_f, kk_f)]
        for x in range(4):
            w_raw.append(y[:, :, 2 * P * x:2 * P * x + P])
            w_low.append(y_r[:, :, 2 * P * x:2 * P * x + P])
            w_hi.append(y_r[:, :, 2 * P * x + P:2 * P * (x + 1)])
        for x in range(2):
            w_raw.append(w_raw_late[:, x])
            w_low.append(w_low_late[:, x])
            w_hi.append(w_hi_late[:, x])

        x_loaded = [sem(f"x_loaded{i}") for i in range(NQ + 1)]
        w_loaded = [sem(f"w_loaded{i}") for i in range(W_SLOTS)]
        const_loaded = sem("const_loaded")
        bf_loaded = sem("bf_loaded")
        g_pre_loaded = sem("g_pre_loaded")
        ident_loaded = sem("ident_loaded")
        neg_c_stored = sem("neg_c_stored")
        neg_c_loaded = sem("neg_c_loaded")
        again_loaded = [sem(f"again_loaded{i}") for i in range(NQ)]
        g_post_loaded = sem("g_post_loaded")
        out_stored = [sem(f"out_stored{i}") for i in range(2)]
        dve_chain = sem("dve_chain")
        high_ready = sem("high_ready")
        low_ready = sem("low_ready")
        stacked = {"kf": sem("fox_keys_stacked"), "qf": sem("fox_queries_stacked"),
                   "qs": sem("swa_queries_stacked"), "ks": sem("swa_keys_stacked")}
        swa_keys_high = sem("swa_keys_high")
        swa_keys_placed = sem("swa_keys_placed")
        x_squared = sem("x_squared")
        x_rooted = sem("x_rooted")
        var_ready = sem("var_ready")
        x_gained = sem("x_gained")
        x_normed = sem("x_normed")
        x_newton = sem("x_newton")
        cleared = sem("cleared")
        u_transposed = sem("u_transposed")
        u_hi_ready = sem("u_hi_ready")
        u_ready = sem("u_ready")
        w_hi_ready = sem("w_hi_ready")
        w_ready = {"pool": sem("w_ready_pool"), "dve": sem("w_ready_dve")}
        chunk_done = sem("chunk_done")
        chunk_drained = sem("chunk_drained")
        z_tanh = sem("z_tanh")
        z_used = sem("z_used")
        f_step = sem("f_step")
        f_back = sem("f_back")
        neg_c_ready = sem("neg_c_ready")
        swa_values_ready = sem("swa_values_ready")
        transposed = sem("transposed")
        group_freed = {"act": sem("group_freed_act"), "dve": sem("group_freed_dve")}
        scored = sem("scored")
        logits_ready = sem("logits_ready")
        exp_done = sem("exp_done")
        normed = sem("normed")
        group_used = sem("group_used")
        y_copied = sem("y_copied")
        y_hi_ready = sem("y_hi_ready")
        y_split = sem("y_split")
        gate_done = sem("gate_done")
        gate_tanh = sem("gate_tanh")
        up_done = sem("up_done")
        up_gated = sem("up_gated")
        m_ready = sem("m_ready")
        m_hi_ready = sem("m_hi_ready")
        m_split = sem("m_split")
        out_done = sem("out_done")
        out_copied = sem("out_copied")
        natural_done = sem("natural_done")
        out_squared = sem("out_squared")
        out_var = sem("out_var")
        out_rooted = sem("out_rooted")
        result_scaled = sem("result_scaled")
        result_ready = {"pool": sem("result_ready_pool"), "dve": sem("result_ready_dve")}

        block = ctx.enter_context(nc.Block())

        first_out = len(entries) - KT

        def slot_of(e):
            if e < 4:
                return e
            if e < first_out:
                return e % 2
            return (first_out % 2, (first_out + 1) % 2, 4, 5, 6, 7, 8, 9)[e - first_out]

        def w_parts(e):
            kind, j = entries[e]
            slot = w_raw[slot_of(e)]
            if kind in ("qs", "zs"):
                base = COL_QA if kind == "qs" else COL_ZA
                return [(slot[:, :, g * HEAD:(g + 1) * HEAD],
                         w_v[:, :, base + (j + PAIRS * g) * HEAD:base + (j + PAIRS * g + 1) * HEAD])
                        for g in range(2)]
            if kind == "up":
                cols = slice(j * P, (j + 1) * P)
                return [(slot[g * HEAD:(g + 1) * HEAD, 0:PAIRS, :], wus_v[g][:, :, cols]) for g in range(2)] + [
                    (slot[:, PAIRS:KT, :], wuf_v[:, :, cols])]
            if kind == "f":
                return [(slot[:, :, 0:F_LOW], w_v[:, :, COL_FF:COL_FF + F_LOW])]
            if kind == "out":
                return [(slot, wo_v[:, :, j * P:(j + 1) * P])]
            base = {"ks": COL_KA, "vs": COL_VA, "qf": COL_QF, "kf": COL_KF, "vf": COL_VF, "zf": COL_ZF,
                    "ga": COL_GA, "gf": COL_GF}[kind] + j * P
            return [(slot, w_v[:, :, base:base + P])]

        slot_count = [0] * W_SLOTS
        slot_user = [None] * W_SLOTS
        w_target, last_in_slot = [], []
        for e in range(len(entries)):
            s = slot_of(e)
            slot_count[s] += 16 * len(w_parts(e))
            w_target.append(slot_count[s])
            last_in_slot.append(slot_user[s])
            slot_user[s] = e

        entry_end, z_number, q_chunk, values_ready, values_chunk = {}, {}, {}, {}, {}
        exps_until = [0]
        low_chunk, low_target = {}, {}
        drained, plain = {}, 0
        for st in steps:
            if st.kind == "project":
                entry_end[st.entry] = (chunk_done, st.k + 1)
                kind, j = st.name
                if kind in ("kf", "qf", "qs"):
                    low_chunk[st.k] = len(low_chunk)
                    low_target[st.name] = 2 * len(low_chunk)
                    drained[st.k] = (low_ready, 2 * len(low_chunk))
                else:
                    plain += 1
                    drained[st.k] = (chunk_drained, plain)
                if kind in ("zs", "zf"):
                    z_number[st.k] = len(z_number)
                if kind in ("qs", "qf"):
                    q_chunk[(kind[1], j)] = st.k
                if kind == "ks":
                    swa_keys_chunk = st.k
                if kind in ("vs", "vf"):
                    values_chunk[st.name] = st.k
            elif st.kind == "gate":
                entry_end[st.entry] = (gate_done, 4 * st.d + 2 * st.b + st.c + 1)
            elif st.kind == "up":
                entry_end[st.entry] = (up_done, 4 * st.d + 2 * st.c + st.b + 1)
            elif st.kind == "out":
                entry_end[st.entry] = (out_done, st.k + 1)
            elif st.kind == "piece" and st.t == 0:
                exps_until.append(exps_until[-1] + (4 if st.n.stage[0] == "s" else 2))
            elif st.kind == "values":
                values_ready[(st.name[0][1], st.name[1])] = {who: v for _, who, v, _ in st.groups}

        by_pool = first_out + 1

        def split_done(e):
            return (w_ready["pool"], e + 1) if e < by_pool else (w_ready["dve"], e - by_pool + 1)

        def groups_now(st):
            return st.groups[:2] if st.kind == "open" else st.n.groups[st.t + 2:st.t + 3]

        def bank4(bank, r):
            return PS[:, bank, :].rearrange("p (k t) -> p k t", k=4)[:, :, 0:r]

        def bank_of(k):
            return PJ_BANK + k % 2 if k >= EARLY_CHUNKS else U_RING + k % 4

        def high_part(st, h):
            part = slice(h * HEAD, (h + 1) * HEAD)
            if st.name[0] == "kf":
                return part, kk_f[part, h, st.t0:st.t0 + st.w]
            return part, (qq_f if st.name[0] == "qf" else qq_s)[part, h, st.t0 - N_META:st.t0 - N_META + st.w]

        def fox_keys_low(j):
            return v_t[:, :].bitcast(F32R) if j else qq_f[:, :, :].rearrange("p a b -> p (a b)")[:, 0:LENGTH]

        def key_places(g, k, half):
            src, dst = k[g * HEAD:(g + 1) * HEAD], kk_s[half * HEAD:(half + 1) * HEAD, g]
            real = src[:, N_META:].rearrange("p (n w) -> p n w", n=NQ)
            meta = src[:, 0:N_META].rearrange("p (o w) -> p o w", o=1).to_broadcast([HEAD, NQ - 1, N_META])
            return [(dst[:, :, A_ROWS:], real), (dst[:, 1:, N_META:A_ROWS], real[:, 0:NQ - 1, CHUNK:]),
                    (dst[:, 0, 0:A_ROWS], src[:, 0:A_ROWS]), (dst[:, 1:, 0:N_META], meta)]

        def store_halves(queue, n, who, before):
            for x in range(2):
                cols = slice(x * BANK, (x + 1) * BANK)
                queue.wait_ge(result_ready[who], before + x + 1)
                queue.dma_start(out_v[n][:, cols], result[:, n % 2, cols]).then_inc(out_stored[n % 2], 16)

        def natural(n):
            return PS[:, 4 + 2 * (n % 2):6 + 2 * (n % 2), :].rearrange("p a b -> p (a b)")

        def values_copies(g, tiles):
            what, n0 = tiles[0]
            bank = PS[:, T_BANK + g % T_RING, :]
            if (what, n0) == ("f", 0):
                return [(v_f[h * HEAD:h * HEAD + N_META, 0, h * HEAD:(h + 1) * HEAD],
                         bank[0:N_META, h * HEAD:(h + 1) * HEAD]) for h in range(2)]
            r = A_ROWS if what == "a" else P
            dst = {"a": v_a, "b": v_b, "f": v_f}[what][0:r, n0:n0 + len(tiles), :]
            return [(dst, bank[0:r, 0:P * len(tiles)].rearrange("p (n d) -> p n d", n=len(tiles)))]

        last_score_of_stage = {}
        for st in steps:
            if st.kind == "piece":
                last_score_of_stage[st.n.stage] = st.n

        CONST_LOADS = 5
        VALUES_COPIES = 3
        KEYS_PLACED = 8

        @block.sync
        def _(sp):
            def load_const(dst, src):
                sp.dma_start(dst, src).then_inc(const_loaded, 16)

            def load_w(e):
                if last_in_slot[e] is not None:
                    sp.wait_ge(*entry_end[last_in_slot[e]])
                elif 4 <= slot_of(e) < 8:
                    sp.wait_ge(m_split, KT if slot_of(e) < 6 else 2 * KT)
                for dst, src in w_parts(e):
                    sp.dma_start(dst, src).then_inc(w_loaded[slot_of(e)], 16)

            def load_x(n):
                if n == 0:
                    sp.dma_start(x_t[0][0:N_META, :], meta_tokens).then_inc(x_loaded[0], 16)
                else:
                    sp.dma_start(x_t[n], x_v[n - 1]).then_inc(x_loaded[n], 16)

            with nc.allow_non_contiguous_dma(reason="small constants"):
                for n in range(3):
                    load_x(n)
                load_w(0)
                for n in range(3, 6):
                    load_x(n)
                sp.dma_start(bf[:, :], b_forget.rearrange("o h -> h o")).then_inc(bf_loaded, 16)
                load_w(1)
                load_x(6)
                load_w(2)
                load_x(7)
                load_x(8)
                load_const(const[:, :], const_in.bitcast(BF16))
                load_const(rows[:, :], rows_in.bitcast(BF16))
                load_const(sink[:, :], sinks.rearrange("o g h -> o (g h)").to_broadcast([P, HEADS]))
                for b in range(2):
                    load_const(half_bg[:, b, :], b_gate[0, b].rearrange("(k p) -> p k", p=P))
                for e in range(3, len(entries)):
                    if slot_of(e) == 8:
                        sp.wait_ge(m_ready, 2 * KT)
                        sp.wait_ge(up_done, 4 * KT)
                        sp.dma_start(g_post_row[:, :], g_post.to_broadcast([P, D_MODEL])).then_inc(g_post_loaded, 16)
                    load_w(e)
                    kind, j = entries[e - 2]
                    if kind == "kf":
                        if j == 0:
                            sp.wait_ge(neg_c_ready, 1)
                            sp.dma_start(neg_c_dram, neg_c_rows).then_inc(neg_c_stored, 16)
                            sp.wait_ge(neg_c_stored, 16)
                        else:
                            sp.wait_ge(logits_ready, last_score_of_stage[("f", j - 1)].last_piece[1] + 1)
                        for h in range(2):
                            sp.dma_start(neg_c[:, h, :], neg_c_dram[2 * j + h:2 * j + h + 1, :].to_broadcast(
                                [P, LENGTH])).then_inc(neg_c_loaded, 16)

                for n in range(NQ):
                    if n >= AGAIN_RING:
                        sp.wait_ge(result_ready["pool"], n - AGAIN_RING + 1)
                    sp.dma_start(x_again[:, n % AGAIN_RING, :], x_v[n]).then_inc(again_loaded[n], 16)
                store_halves(sp, NQ - 1, "dve", 0)

        @block.gpsimd
        def _(pool):
            def split_lo(e):
                s = slot_of(e)
                pool.wait_ge(w_hi_ready, e + 1)
                if entries[e][0] == "f":
                    cols = slice(0, HEADS)
                    nc.gpsimd.tensor_tensor(w_hi[s][:, :, F_LOW:F_LOW + HEADS], w_raw[s][:, :, cols],
                                            w_hi[s][:, :, cols].bitcast(F32),
                                            ALU.subtract).then_inc(w_ready["pool"], 1)
                    return
                nc.gpsimd.tensor_tensor(w_low[s], w_raw[s], w_hi[s].bitcast(F32),
                                        ALU.subtract).then_inc(w_ready["pool"], 1)

            for st in steps:
                if st.kind == "split_w" and st.entry < by_pool:
                    split_lo(st.entry)
                if st.kind == "drain" and st.n.last and st.n.name[0] in ("kf", "qf", "qs"):
                    kind, j = st.n.name
                    pool.wait_ge(low_ready, low_target[(kind, j)])
                    for h in range(2):
                        here, there = slice(h * HEAD, (h + 1) * HEAD), slice((1 - h) * HEAD, (2 - h) * HEAD)
                        if kind == "kf":
                            dst, src = kk_f[there, h, :], fox_keys_low(j)[here, :]
                        else:
                            qq = qq_f if kind == "qf" else qq_s
                            dst, src = qq[there, h, :], qq[here, h, :]
                        pool.dma_start(dst, src).then_inc(stacked[kind], 16)
                if st.kind == "place_keys":
                    g = st.t
                    if g == 0:
                        pool.wait_ge(*drained[swa_keys_chunk])
                    for to, what in key_places(g, k_s_lo, 1 - g):
                        pool.dma_start(to, what).then_inc(stacked["ks"], 16)
                if st.kind == "u_square" and st.n in POOL_GAINS:
                    if st.n == POOL_GAINS[0]:
                        pool.wait_ge(g_pre_loaded, 16)
                    pool.wait_ge(x_squared, st.n + 1)
                    nc.gpsimd.tensor_tensor(x_t[st.n], x_t[st.n], g_pre_row[:, :], ALU.mult).then_inc(x_gained, 1)
                if st.kind == "finish" and st.n < NQ - 1:
                    n = st.n
                    pool.wait_ge(again_loaded[n], 16)
                    for x in range(1 if n < NQ - 2 else 2):
                        cols = slice(0, D_MODEL) if n < NQ - 2 else slice(x * BANK, (x + 1) * BANK)
                        pool.wait_ge(result_scaled, n + x + 1)
                        nc.gpsimd.tensor_tensor(result[:, n % 2, cols], result[:, n % 2, cols],
                                                x_again[:, n % AGAIN_RING, cols],
                                                ALU.add).then_inc(result_ready["pool"], 1)
                if st.kind == "up" and st.b == 1:
                    pool.wait_ge(up_gated, 4 * st.d + 2 * st.c + 2)
                    nc.gpsimd.tensor_tensor(y[:, st.d, st.c * BANK:(st.c + 1) * BANK], gated[:, 0, st.c, :],
                                            gated[:, 1, st.c, :], ALU.add).then_inc(m_ready, 1)

        @block.scalar
        def _(act):
            def split_hi(e):
                s = slot_of(e)
                act.wait_ge(w_loaded[s], w_target[e])
                cols = slice(0, F_LOW if entries[e][0] == "f" else P)
                nc.scalar.activation(w_hi[s][:, :, cols], w_raw[s][:, :, cols], ACT.Copy).then_inc(w_hi_ready, 1)

            with nc.allow_non_contiguous_dma(reason="a broadcast row"):
                act.dma_start(g_pre_row, g_pre.to_broadcast([P, D_MODEL])).then_inc(g_pre_loaded, 16)
                act.dma_start(ident[:, :], ident_in).then_inc(ident_loaded, 16)

            def store(n):
                act.wait_ge(result_ready["pool"], n + 1)
                act.dma_start(out_v[n], result[:, n % 2, :]).then_inc(out_stored[n % 2], 16)

            act.wait_ge(cleared, 1)
            nc.scalar.activation(stat[:, 9, 0:1], stat[:, 9, 1:2], ACT.Sqrt).then_inc(x_rooted, 1)
            for st in steps:
                if st.kind == "split_w":
                    split_hi(st.entry)
                elif st.kind == "u_square":
                    n = st.n
                    r = N_META if n == 0 else P
                    act.wait_ge(x_loaded[n], 16)
                    if n:
                        act.wait_ge(x_squared, n)
                    nc.scalar.activation(squares[0:r, :], x_t[n][0:r, :], ACT.Square,
                                         accum_out=stat[0:r, 0, n:n + 1]).then_inc(x_squared, 1)
                elif st.kind == "u_var":
                    n = st.n
                    act.wait_ge(var_ready, n + 1)
                    nc.scalar.activation(stat[:, 2, n:n + 1], stat[:, 1, n:n + 1], ACT.Sqrt).then_inc(x_rooted, 1)
                elif st.kind == "u_copy":
                    n = st.n
                    r = N_META if n == 0 else P
                    c0 = 0 if n == 0 else N_META + (n - 1) * P
                    for g in range(2 * n, 2 * n + 2):
                        k0 = 4 * (g % 2)
                        act.wait_ge(u_transposed, g + 1)
                        nc.scalar.activation(u_hi[:, k0:k0 + 4, c0:c0 + r], bank4(g % U_RING, r),
                                             ACT.Copy).then_inc(u_hi_ready, 1)
                elif st.kind == "forget" and st.t == 0:
                    act.wait_ge(f_step, 1)
                    nc.scalar.activation(f_e, f_e, ACT.Exp, scale=-1.0).then_inc(f_back, 1)
                    act.wait_ge(f_back, 1)
                    nc.scalar.activation(f_e, f_e, ACT.Ln, bias=1.0).then_inc(f_back, 1)
                elif st.kind == "drain":
                    st = st.n
                    kind = st.name[0]
                    src = PS[:, bank_of(st.k), 0:st.w]
                    if kind not in ("f", "vs", "vf"):
                        act.wait_ge(chunk_done, st.k + 1)
                    if kind in ("zs", "zf"):
                        z_no = z_number[st.k]
                        if z_no:
                            act.wait_ge(z_used, z_no)
                        nc.scalar.activation(z_t[:, 0:st.w], src, ACT.Tanh, scale=0.5).then_inc(z_tanh, 1)
                    elif kind == "ks":
                        nc.scalar.activation(k_s_hi[:, st.t0:st.t0 + st.w], src, ACT.Copy).then_inc(swa_keys_high, 1)
                    elif kind in ("kf", "qf", "qs"):
                        if st.name == ("qf", 0) and st.c == 0:
                            act.wait_ge(stacked["kf"], 32)
                        for h in range(2):
                            part, dst = high_part(st, h)
                            nc.scalar.activation(dst, src[part, :], ACT.Copy,
                                                 scale=1.0 if kind == "kf" else SCALE).then_inc(high_ready, 1)
                elif st.kind == "values":
                    for g, who, v, tiles in st.groups:
                        if who == "act":
                            act.wait_ge(transposed, g + 1)
                            for dst, src in values_copies(g, tiles):
                                ins = nc.scalar.activation(dst, src, ACT.Copy)
                            ins.then_inc(group_freed["act"], 1)
                elif st.kind == "piece":
                    k, st = st.n.first_piece + st.t, st.n
                    b = st.i % 2
                    for h in range(2):
                        if k != st.last_piece[h]:
                            continue
                        act.wait_ge(logits_ready, k + 1)
                        x_last = max(q[1] for q in st.pieces)
                        width = max(q[2] + q[3] for q in st.pieces)
                        bias = neg_max[:, b, h, x_last:x_last + 1]
                        nc.scalar.activation(probs_ring[b][:, h, 0:width], probs_ring[b][:, h, 0:width], ACT.Exp,
                                             bias=bias, scale=-1.0, accum_out=den[:, b, h:h + 1]).then_inc(exp_done, 1)
                        if st.stage[0] == "s":
                            hh = st.stage[1] + PAIRS * h
                            nc.scalar.activation(es[:, b, h:h + 1], sink[:, hh:hh + 1], ACT.Exp,
                                                 bias=bias).then_inc(exp_done, 1)
                elif st.kind in ("open", "pv"):
                    for g, pg, who, v, tiles in groups_now(st):
                        if who == "act":
                            act.wait_ge(transposed, g + 1)
                            if pg >= PT_RING:
                                act.wait_ge(group_used, pg - PT_RING + 1)
                            nc.scalar.activation(p_t[:, pg % PT_RING, 0:P * len(tiles)],
                                                 PS[:, T_BANK + g % T_RING, 0:P * len(tiles)],
                                                 ACT.Copy).then_inc(group_freed["act"], 1)
                elif st.kind == "split_y":
                    for s in range(2 * PAIRS):
                        nc.scalar.activation(y_hi[:, s, :], y[:, s, :], ACT.Copy).then_inc(y_hi_ready, 1)
                elif st.kind == "gate":
                    k = 4 * st.d + 2 * st.b + st.c
                    if k == 0:
                        act.wait_ge(group_used, totals["pgroups"])
                        act.wait_ge(z_used, len(z_number))
                    act.wait_ge(gate_done, k + 1)
                    if st.d:
                        act.wait_ge(up_gated, 4 * (st.d - 1) + 2 * st.c + st.b + 1)
                    nc.scalar.activation(tanh_g[:, st.b, st.c, :], PS[:, 2 * st.b + st.c, :], ACT.Tanh, scale=0.5,
                                         bias=half_bg[:, st.b, st.d:st.d + 1]).then_inc(gate_tanh, 1)
                elif st.kind == "split_m":
                    if st.k == 0:
                        act.wait_ge(gate_done, 4 * KT)
                    act.wait_ge(m_ready, 2 * st.d + st.c + 1)
                    tok = slice(st.c * BANK, (st.c + 1) * BANK)
                    nc.scalar.activation(m_hi[:, st.d, tok], y[:, st.d, tok], ACT.Copy,
                                         scale=0.5).then_inc(m_hi_ready, 1)
                elif st.kind == "out":
                    act.wait_ge(out_done, st.k + 1)
                    if st.half >= 2:
                        act.wait_ge(natural_done, 2 * OUT_GROUPS[st.half - 1][0])
                    nc.scalar.activation(o_t[:, st.half % 2, st.d, 0:st.w], PS[:, st.k % 4, 0:st.w],
                                         ACT.Copy).then_inc(out_copied, 1)
                elif st.kind == "natural":
                    n, half = st.n, st.half
                    if n == NQ - 2 and half == 0:
                        store(n - 1)
                    act.wait_ge(natural_done, st.k + 1)
                    if st.k:
                        act.wait_ge(out_squared, st.k)
                    nc.scalar.activation(squares2[:, :], natural(n)[:, half * BANK:(half + 1) * BANK], ACT.Square,
                                         accum_out=stat[:, (4, 8)[half], n:n + 1]).then_inc(out_squared, 1)
                elif st.kind == "root":
                    n = st.n
                    act.wait_ge(out_var, n + 1)
                    nc.scalar.activation(stat[:, 6, n:n + 1], stat[:, 5, n:n + 1], ACT.Sqrt).then_inc(out_rooted, 1)
                elif st.kind == "finish" and 0 < st.n < NQ - 2:
                    store(st.n - 1)

            store_halves(act, NQ - 2, "pool", NQ - 2)
            act.wait_ge(out_stored[0], 16 * (NQ // 2 + 1))
            act.wait_ge(out_stored[1], 16 * (NQ // 2 + 1))

        @block.vector
        def _(dve):
            chain = [0]

            def link(ins):
                chain[0] += 1
                ins.then_inc(dve_chain, 1)
                dve.wait_ge(dve_chain, chain[0])

            def root(base, n):
                b, h, t = (stat[:, base + x, n:n + 1] for x in (1, 2, 3))
                link(nc.vector.reciprocal(t, h))
                link(nc.vector.scalar_tensor_tensor(out=t, in0=t, scalar=b, in1=h, op0=ALU.mult, op1=ALU.add))
                return nc.vector.reciprocal(t, t)

            def norm(st):
                b = st.i % 2
                dve.wait_ge(exp_done, exps_until[st.i + 1])
                if st.stage[0] == "s":
                    link(nc.vector.tensor_tensor(den[:, b, :], den[:, b, :], es[:, b, :], ALU.add))
                link(nc.vector.reciprocal(rec[:, b, :], den[:, b, :]))
                if st.stage[0] == "f":
                    scale = rec[:, b, :].rearrange("p (h o) -> p h o", o=1).to_broadcast([P, 2, N_META])
                    nc.vector.tensor_tensor(meta_probs[:, b, :].rearrange("p (h c) -> p h c", h=2)[:, :, 0:N_META],
                                            probs_ring[b][:, :, 0:N_META], scale, ALU.mult)
                own = slice(0 if st.stage[0] == "s" else N_META, max(q[2] + q[3] for q in st.pieces))
                for h in range(2):
                    nc.vector.tensor_scalar(probs_ring[b][:, h, own], probs_ring[b][:, h, own],
                                            rec[:, b, h:h + 1], None, ALU.mult).then_inc(normed, 1)

            nc.vector.memset(stat[:, :, :], 1.0).then_inc(cleared, 1)
            nc.vector.memset(f_ones, 1.0).then_inc(cleared, 1)
            nc.vector.memset(v_f[:, 0, :], 0.0).then_inc(cleared, 1)
            nc.vector.memset(meta_probs[:, :, :], 0.0).then_inc(cleared, 1)
            for st in steps:
                if st.kind == "split_w" and st.entry >= by_pool:
                    s = slot_of(st.entry)
                    dve.wait_ge(w_hi_ready, st.entry + 1)
                    nc.vector.tensor_tensor(w_low[s], w_raw[s], w_hi[s].bitcast(F32),
                                            ALU.subtract).then_inc(w_ready["dve"], 1)
                elif st.kind == "u_var":
                    n = st.n
                    dve.wait_ge(x_squared, n + 1)
                    nc.vector.tensor_scalar(stat[:, 1, n:n + 1], stat[:, 0, n:n + 1], 0.25 / D_MODEL, 0.25 * EPS,
                                            ALU.mult, ALU.add).then_inc(var_ready, 1)
                elif st.kind == "u_newton":
                    dve.wait_ge(x_rooted, st.n + 2)
                    root(0, st.n).then_inc(x_newton, 1)
                elif st.kind == "u_norm":
                    n = st.n
                    r = N_META if n == 0 else P
                    if n == 0:
                        dve.wait_ge(g_pre_loaded, 16)
                    dve.wait_ge(x_newton, n + 1)
                    if n in POOL_GAINS:
                        dve.wait_ge(x_gained, POOL_GAINS.index(n) + 1)
                        nc.vector.tensor_scalar(x_t[n], x_t[n], stat[:, 3, n:n + 1], None,
                                                ALU.mult).then_inc(x_normed, 1)
                        continue
                    nc.vector.scalar_tensor_tensor(out=x_t[n][0:r, :], in0=x_t[n][0:r, :],
                                                   scalar=stat[0:r, 3, n:n + 1], in1=g_pre_row[0:r, :], op0=ALU.mult,
                                                   op1=ALU.mult).then_inc(x_normed, 1)
                elif st.kind == "u_lo":
                    n = st.n
                    r = N_META if n == 0 else P
                    c0 = 0 if n == 0 else N_META + (n - 1) * P
                    g = 2 * n + st.t
                    k0 = 4 * st.t
                    dve.wait_ge(u_hi_ready, g + 1)
                    nc.vector.tensor_tensor(u_lo[:, k0:k0 + 4, c0:c0 + r], bank4(g % U_RING, r),
                                            u_hi[:, k0:k0 + 4, c0:c0 + r].bitcast(F32),
                                            ALU.subtract).then_inc(u_ready, 1)
                elif st.kind == "drain":
                    st = st.n
                    kind = st.name[0]
                    src = PS[:, bank_of(st.k), 0:st.w]
                    dve.wait_ge(chunk_done, st.k + 1)
                    if kind == "f":
                        dve.wait_ge(bf_loaded, 16)
                        tok = slice(st.t0, st.t0 + st.w)
                        link(nc.vector.tensor_scalar(f_x[:, tok], src[0:HEADS, :], bf[:, 0:1], None, ALU.add))
                        nc.vector.tensor_tensor(f_x[:, tok], f_x[:, tok], src[F_LOW:F_LOW + HEADS, :],
                                                ALU.add).then_inc(chunk_drained, 1)
                    elif kind == "ks":
                        tok = slice(st.t0, st.t0 + st.w)
                        dve.wait_ge(swa_keys_high, st.c + 1)
                        nc.vector.tensor_tensor(k_s_lo[:, tok], src, k_s_hi[:, tok].bitcast(F32),
                                                ALU.subtract).then_inc(chunk_drained, 1)
                    elif kind in ("qf", "qs", "kf"):
                        for h in range(2):
                            part, hi = high_part(st, h)
                            if kind == "kf":
                                lo = fox_keys_low(st.name[1])[part, st.t0:st.t0 + st.w]
                            else:
                                lo = (q_lo if kind == "qf" else q_lo_s)[part, st.t0 - N_META:st.t0 - N_META + st.w]
                            dve.wait_ge(high_ready, low_chunk[st.k] * 2 + h + 1)
                            ins = nc.vector.scalar_tensor_tensor(out=lo, in0=src[part, :],
                                                                 scalar=1.0 if kind == "kf" else SCALE,
                                                                 in1=hi.bitcast(F32), op0=ALU.mult, op1=ALU.subtract)
                            ins.then_inc(low_ready, 1)
                    elif kind in ("vs", "vf"):
                        if kind == "vf" and st.c == 0:
                            dve.wait_ge(stacked["kf"], 32 * (st.name[1] + 1))
                        nc.vector.tensor_copy(v_t[:, st.t0:st.t0 + st.w], src).then_inc(chunk_drained, 1)
                        if kind == "vs" and st.last:
                            dve.wait_ge(*drained[st.k])
                            real = v_t[:, N_META:].rearrange("p (n w) -> p n w", n=NQ)
                            meta = v_t[:, 0:N_META].rearrange("p (o w) -> p o w", o=1).to_broadcast([P, NQ, N_META])
                            nc.vector.memset(v_a_t[:, 0, N_META:], 0.0).then_inc(swa_values_ready, 1)
                            nc.vector.tensor_copy(v_a_t[:, 1:, N_META:], real[:, 0:NQ - 1, CHUNK:]
                                                  ).then_inc(swa_values_ready, 1)
                            nc.vector.tensor_copy(v_a_t[:, :, 0:N_META], meta).then_inc(swa_values_ready, 1)
                    else:
                        slot = st.name[1] + (0 if kind == "zs" else PAIRS)
                        yy = y[:, slot, st.t0 - N_META:st.t0 - N_META + st.w]
                        zz = z_t[:, 0:st.w]
                        dve.wait_ge(z_tanh, z_number[st.k] + 1)
                        ins = nc.vector.scalar_tensor_tensor(out=zz, in0=zz, scalar=1.0, in1=src, op0=ALU.add,
                                                             op1=ALU.mult)
                        ins.then_inc(chunk_drained, 1)
                        dve.wait_ge(*drained[st.k])
                        nc.vector.scalar_tensor_tensor(out=yy, in0=zz, scalar=0.5, in1=yy, op0=ALU.mult,
                                                       op1=ALU.mult).then_inc(z_used, 1)
                elif st.kind == "place_keys":
                    for to, what in key_places(st.t, k_s_hi, st.t):
                        dve.wait_ge(*drained[swa_keys_chunk])
                        nc.vector.tensor_copy(to, what.bitcast(F32)).then_inc(swa_keys_placed, 1)
                elif st.kind == "forget" and st.t == 0:
                    dve.wait_ge(const_loaded, 16 * CONST_LOADS)
                    nc.vector.tensor_scalar(half_bg[:, :, :], half_bg[:, :, :], 0.5, None, ALU.mult
                                            ).then_inc(cleared, 1)
                    nc.vector.tensor_scalar(neg_sink[:, :], sink[:, :], -1.0, None, ALU.mult).then_inc(cleared, 1)
                    dve.wait_ge(cleared, 6)
                    dve.wait_ge(*drained[2 * len(EARLY_TOKENS) - 2])
                    nc.vector.scalar_tensor_tensor(out=f_e, in0=f_x, scalar=-1.0, in1=f_x, op0=ALU.mult,
                                                   op1=ALU.max).then_inc(f_step, 1)
                    link(nc.vector.tensor_scalar(f_x, f_x, -1.0, 0.0, ALU.mult, ALU.max))
                elif st.kind == "forget":
                    dve.wait_ge(f_back, 2)
                    link(nc.vector.tensor_tensor(f_x, f_x, f_e, ALU.add))
                    nc.vector.tensor_tensor_scan(neg_c_rows, f_ones, f_x, 0.0, ALU.mult,
                                                 ALU.add).then_inc(neg_c_ready, 1)
                elif st.kind == "values":
                    for g, who, v, tiles in st.groups:
                        if who == "dve":
                            dve.wait_ge(transposed, g + 1)
                            for dst, src in values_copies(g, tiles):
                                ins = nc.vector.tensor_copy(dst, src)
                            ins.then_inc(group_freed["dve"], 1)
                elif st.kind == "piece":
                    y_, st = st.t, st.n
                    b = st.i % 2
                    swa = st.stage[0] == "s"
                    if st.i >= 2 and y_ == 0:
                        dve.wait_ge(transposed, items_done_groups[st.i - 2][0] + 1)
                    if not swa and st.t == 0 and y_ == 0:
                        dve.wait_ge(neg_c_loaded, 32 * (st.stage[1] + 1))
                    h, x_, c0, w = st.pieces[y_]
                    k = st.first_piece + y_
                    hh = st.stage[1] + PAIRS * h
                    dve.wait_ge(scored, k + 1)
                    if x_:
                        dve.wait_ge(logits_ready, k - 1)
                    init = neg_max[:, b, h, x_ - 1:x_] if x_ else (neg_sink[:, hh:hh + 1] if swa else BIG)
                    in1 = alibi[:, hh, :] if swa else neg_c[:, h, c0:c0 + w]
                    nc.vector.tensor_tensor_reduce(probs_ring[b][:, h, c0:c0 + w],
                                                   PS[:, S_BANK + k % S_RING, 0:w], in1, -1.0, init,
                                                   ALU.add, ALU.min,
                                                   neg_max[:, b, h, x_:x_ + 1]).then_inc(logits_ready, 1)
                elif st.kind == "norm":
                    norm(st.n)
                elif st.kind in ("open", "pv"):
                    for g, pg, who, v, tiles in groups_now(st):
                        if who == "dve":
                            dve.wait_ge(transposed, g + 1)
                            if pg >= PT_RING:
                                dve.wait_ge(group_used, pg - PT_RING + 1)
                            nc.vector.tensor_copy(p_t[:, pg % PT_RING, 0:P * len(tiles)],
                                                  PS[:, T_BANK + g % T_RING, 0:P * len(tiles)]
                                                  ).then_inc(group_freed["dve"], 1)
                elif st.kind == "y_copy":
                    dve.wait_ge(group_used, st.groups[-1][1] + 1)
                    slot = st.stage[1] + (0 if st.stage[0] == "s" else PAIRS)
                    nc.vector.tensor_copy(y[:, slot, st.t * P:(st.t + 1) * P],
                                          PS[:, Y_BANK, 0:P]).then_inc(y_copied, 1)
                elif st.kind == "split_y":
                    for s in range(2 * PAIRS):
                        dve.wait_ge(y_hi_ready, s + 1)
                        nc.vector.tensor_tensor(y_lo[:, s, :], y[:, s, :], y_hi[:, s, :].bitcast(F32),
                                                ALU.subtract).then_inc(y_split, 1)
                elif st.kind == "up":
                    dve.wait_ge(up_done, 4 * st.d + 2 * st.c + st.b + 1)
                    dve.wait_ge(gate_tanh, 4 * st.d + 2 * st.b + st.c + 1)
                    if st.d:
                        dve.wait_ge(m_ready, 2 * (st.d - 1) + st.c + 1)
                    nc.vector.scalar_tensor_tensor(out=gated[:, st.b, st.c, :], in0=tanh_g[:, st.b, st.c, :],
                                                   scalar=1.0, in1=PS[:, 4 + 2 * st.b + st.c, :], op0=ALU.add,
                                                   op1=ALU.mult).then_inc(up_gated, 1)
                elif st.kind == "split_m":
                    dve.wait_ge(m_hi_ready, st.k + 1)
                    tok = slice(st.c * BANK, (st.c + 1) * BANK)
                    nc.vector.scalar_tensor_tensor(out=m_lo[:, st.d, tok], in0=y[:, st.d, tok], scalar=0.5,
                                                   in1=m_hi[:, st.d, tok].bitcast(F32), op0=ALU.mult,
                                                   op1=ALU.subtract).then_inc(m_split, 1)
                elif st.kind == "natural":
                    n = st.n
                    dve.wait_ge(out_squared, st.k + 1)
                    if st.half == 0:
                        link(nc.vector.tensor_scalar(stat[:, 9, n:n + 1], stat[:, 4, n:n + 1], 0.25 / D_MODEL,
                                                     0.25 * EPS, ALU.mult, ALU.add))
                    else:
                        nc.vector.scalar_tensor_tensor(out=stat[:, 5, n:n + 1], in0=stat[:, 8, n:n + 1],
                                                       scalar=0.25 / D_MODEL, in1=stat[:, 9, n:n + 1], op0=ALU.mult,
                                                       op1=ALU.add).then_inc(out_var, 1)
                elif st.kind == "root":
                    dve.wait_ge(out_rooted, st.n + 1)
                    link(root(4, st.n))
                elif st.kind == "finish":
                    n = st.n
                    if n == 0:
                        dve.wait_ge(g_post_loaded, 16)
                    if n >= 2:
                        dve.wait_ge(out_stored[n % 2], 16 * (n // 2))
                    for x in range(1 if n < NQ - 2 else 2):
                        cols = slice(0, D_MODEL) if n < NQ - 2 else slice(x * BANK, (x + 1) * BANK)
                        nc.vector.scalar_tensor_tensor(out=result[:, n % 2, cols], in0=natural(n)[:, cols],
                                                       scalar=stat[:, 7, n:n + 1], in1=g_post_row[:, cols],
                                                       op0=ALU.mult, op1=ALU.mult).then_inc(result_scaled, 1)
                    if n == NQ - 1:
                        dve.wait_ge(again_loaded[n], 16)
                        for x in range(2):
                            cols = slice(x * BANK, (x + 1) * BANK)
                            dve.wait_ge(result_scaled, n + 2 + x)
                            nc.vector.tensor_tensor(result[:, n % 2, cols], result[:, n % 2, cols],
                                                    x_again[:, n % AGAIN_RING, cols],
                                                    ALU.add).then_inc(result_ready["dve"], 1)

        @block.tensor
        def _(pe):
            def three(dst, e, k, hi, lo, first, last):
                s = slot_of(e)
                pe.matmul(dst, w_hi[s][:, k, :], hi, start=first, stop=False)
                pe.matmul(dst, w_hi[s][:, k, :], lo, start=False, stop=False)
                return pe.matmul(dst, w_low[s][:, k, :], hi, start=False, stop=last)

            def free_bank_of(g):
                if g >= T_RING:
                    who, v = owner[g - T_RING]
                    pe.wait_ge(group_freed[who], v)

            pe.wait_ge(ident_loaded, 16)
            for st in steps:
                if st.kind in ("project", "gate", "up", "out"):
                    pe.wait_ge(*split_done(st.entry))
                if st.kind == "u_norm":
                    n = st.n
                    r = N_META if n == 0 else P
                    pe.wait_ge(x_normed, n + 1)
                    for g in range(2 * n, 2 * n + 2):
                        if g >= U_RING:
                            pe.wait_ge(u_ready, g - U_RING + 1)
                        for j in range(4):
                            k = 4 * (g % 2) + j
                            ins = pe.transpose(PS[:, g % U_RING, j * P:j * P + r],
                                               x_t[n][0:r, k * P:(k + 1) * P], ident[0:r, 0:r])
                        ins.then_inc(u_transposed, 1)
                elif st.kind == "project":
                    tiles = -(-(st.t0 + st.w - N_META) // P) + 1
                    pe.wait_ge(u_ready, 2 * tiles)
                    if st.k >= 4:
                        pe.wait_ge(*drained[st.k - (4 if st.k < EARLY_CHUNKS else 2)])
                    dst = PS[:, bank_of(st.k), 0:st.w]
                    tok = slice(st.t0, st.t0 + st.w)
                    for k in range(KT):
                        if st.name[0] == "f":
                            w = w_hi[slot_of(st.entry)]
                            if k:
                                pe.matmul(PS[0:HEADS, bank_of(st.k), 0:st.w], w[:, k - 1, 0:HEADS],
                                          u_lo[:, k - 1, tok], start=False, stop=False)
                            if k == KT - 1:
                                pe.matmul(PS[0:HEADS, bank_of(st.k), 0:st.w], w[:, k, 0:HEADS], u_lo[:, k, tok],
                                          start=False, stop=False)
                            ins = pe.matmul(PS[0:F_LOW + HEADS, bank_of(st.k), 0:st.w], w[:, k, 0:F_LOW + HEADS],
                                            u_hi[:, k, tok], start=k == 0, stop=k == KT - 1)
                            continue
                        ins = three(dst, st.entry, k, u_hi[:, k, tok], u_lo[:, k, tok], k == 0, k == KT - 1)
                    ins.then_inc(chunk_done, 1)
                elif st.kind == "values":
                    swa = st.name[0] == "vs"
                    pe.wait_ge(*drained[values_chunk[st.name]])
                    if swa:
                        pe.wait_ge(swa_values_ready, VALUES_COPIES)
                    for g, who, v, tiles in st.groups:
                        free_bank_of(g)
                        for j, (what, n) in enumerate(tiles):
                            if what == "a":
                                src, r = v_a_t[:, n, :], A_ROWS
                            elif what == "b" or n:
                                m = n if what == "b" else n - 1
                                src, r = v_t[:, N_META + m * P:N_META + (m + 1) * P], P
                            else:
                                src, r = v_t[:, 0:P], P
                            ins = pe.transpose(PS[0:r, T_BANK + g % T_RING, j * P:(j + 1) * P], src, ident[:, :])
                        ins.then_inc(transposed, 1)
                elif st.kind == "piece":
                    y_, st = st.t, st.n
                    swa = st.stage[0] == "s"
                    if y_ == 0:
                        if swa:
                            pe.wait_ge(stacked["ks"], 16 * KEYS_PLACED)
                            pe.wait_ge(swa_keys_placed, KEYS_PLACED)
                            pe.wait_ge(stacked["qs"], 32 * (st.stage[1] + 1))
                        else:
                            for kind in ("kf", "qf"):
                                pe.wait_ge(stacked[kind], 32 * (st.stage[1] + 1))
                    if st.i == 0:
                        pe.wait_ge(u_ready, 2 * (NQ + 1))
                    h, x_, c0, w = st.pieces[y_]
                    k = st.first_piece + y_
                    hh = st.stage[1] + PAIRS * h
                    if k >= S_RING:
                        pe.wait_ge(logits_ready, k - S_RING + 1)
                    bank = PS[:, S_BANK + k % S_RING, :]
                    rows_ = slice(h * HEAD, (h + 1) * HEAD)
                    more = swa or c0 + w == N_META + (st.t + 1) * P
                    tok = slice(st.t * P, (st.t + 1) * P)
                    qq, lo = (qq_s, q_lo_s) if swa else (qq_f, q_lo)
                    kk = kk_s[:, h, st.t, :] if swa else kk_f[:, h, c0:c0 + w]
                    pe.matmul(bank[:, 0:w], qq[:, h, tok], kk, start=True, stop=False)
                    ins = pe.matmul(bank[:, 0:w], lo[rows_, tok], kk[rows_, :], start=False, stop=not more)
                    if swa and st.t == 0:
                        ins = pe.matmul(bank[:, 0:A_ROWS], ones_row, first_block_row, start=False, stop=True)
                    elif swa:
                        ins = pe.matmul(bank[:, 0:N_META], ones_row,
                                        meta_far_row[:, hh, st.t:st.t + 1].to_broadcast([1, N_META]), start=False,
                                        stop=True)
                    elif more:
                        ins = pe.matmul(bank[:, w - P:w], ident_b, causal, start=False, stop=True)
                    ins.then_inc(scored, 1)
                elif st.kind in ("open", "pv"):
                    number_, st = st.t, st.n if st.kind == "pv" else st
                    opening = st.kind == "open"
                    b = st.i % 2
                    swa = st.stage[0] == "s"

                    def transposes(n):
                        g, pg, who, v, tiles = st.groups[n]
                        free_bank_of(g)
                        for j, (h, x_, c0, w) in enumerate(tiles):
                            pe.wait_ge(normed, 2 * st.i + min(h, 1) + 1)
                            src = meta_probs[:, b, :] if h == BOTH else probs_ring[b][:, h, c0:c0 + w]
                            ins = pe.transpose(PS[0:w, T_BANK + g % T_RING, j * P:(j + 1) * P], src, ident[:, :])
                        ins.then_inc(transposed, 1)

                    def values(n):
                        g, pg, who, v, tiles = st.groups[n]
                        pe.wait_ge(group_freed[who], v)
                        for j, (h, x_, c0, w) in enumerate(tiles):
                            if h == BOTH:
                                ins = pe.matmul(PS[:, Y_BANK, 0:P], v_f[:, 0, :],
                                                p_t[:, pg % PT_RING, j * P:(j + 1) * P],
                                                start=True, stop=False)
                                continue
                            cols = slice(h * HEAD, (h + 1) * HEAD)
                            vv = (v_a, v_b)[x_][0:w, st.t, cols] if swa else v_f[0:w, x_, cols]
                            ins = pe.matmul(PS[h * HEAD:(h + 1) * HEAD, Y_BANK, 0:P], vv,
                                            p_t[0:w, pg % PT_RING, j * P:(j + 1) * P], start=swa and x_ == 0,
                                            stop=x_ == st.n_tiles - 1)
                        ins.then_inc(group_used, 1)

                    if opening:
                        for n in range(len(st.groups[:2])):
                            transposes(n)
                        continue
                    n = number_
                    if n == 0 and st.i:
                        pe.wait_ge(y_copied, st.i)
                    if n == 0 and st.t == 0:
                        for w_, v_ in values_ready[("s", 0) if swa else st.stage].items():
                            pe.wait_ge(group_freed[w_], v_)
                    values(n)
                    if n + 2 < len(st.groups):
                        transposes(n + 2)
                elif st.kind == "gate":
                    if st.d:
                        pe.wait_ge(gate_tanh, 4 * (st.d - 1) + 2 * st.b + st.c + 1)
                    tok = slice(N_META + st.c * BANK, N_META + (st.c + 1) * BANK)
                    for k in range(KT):
                        ins = three(PS[:, 2 * st.b + st.c, :], st.entry, k, u_hi[:, k, tok], u_lo[:, k, tok],
                                    k == 0, k == KT - 1)
                    ins.then_inc(gate_done, 1)
                elif st.kind == "up":
                    if st.d == 0:
                        pe.wait_ge(y_split, PAIRS * (st.b + 1))
                        pe.wait_ge(*drained[totals["chunks"] - 1])
                        pe.wait_ge(y_copied, totals["items"])
                    if st.d:
                        pe.wait_ge(up_gated, 4 * (st.d - 1) + 2 * st.c + st.b + 1)
                    tok = slice(st.c * BANK, (st.c + 1) * BANK)
                    for j in range(PAIRS):
                        k = PAIRS * st.b + j
                        ins = three(PS[:, 4 + 2 * st.b + st.c, :], st.entry, k, y_hi[:, k, tok], y_lo[:, k, tok],
                                    j == 0, j == PAIRS - 1)
                    ins.then_inc(up_done, 1)
                elif st.kind == "out":
                    if st.k == 0:
                        pe.wait_ge(gate_tanh, 4 * KT)
                    if st.k == KT:
                        pe.wait_ge(m_split, 2 * KT)
                    if st.k >= 4:
                        pe.wait_ge(out_copied, st.k - 3)
                    tok = slice(st.t0, st.t0 + st.w)
                    for k in range(KT):
                        if st.k == 0:
                            pe.wait_ge(m_split, k + 1)
                        ins = three(PS[:, st.k % 4, 0:st.w], st.entry, k, m_hi[:, k, tok], m_lo[:, k, tok], k == 0,
                                    k == KT - 1)
                    ins.then_inc(out_done, 1)
                elif st.kind == "natural":
                    n = st.n
                    g = sum(1 for n0, _ in OUT_GROUPS if n0 <= n) - 1
                    if st.k == 0:
                        pe.wait_ge(up_gated, 4 * KT)
                    pe.wait_ge(out_copied, KT * g + 4 * (st.half + 1))
                    if n >= 2:
                        pe.wait_ge(result_scaled, n - 1)
                    t = n - OUT_GROUPS[g][0]
                    for d in range(4 * st.half, 4 * st.half + 4):
                        ins = pe.transpose(PS[:, 4 + 2 * (n % 2) + d // 4, (d % 4) * P:(d % 4 + 1) * P],
                                           o_t[:, g % 2, d, t * P:(t + 1) * P], ident[:, :])
                    ins.then_inc(natural_done, 1)


_INS = ["x", "meta_tokens", "g_pre", "w_in", "b_forget", "b_gate", "sinks", "w_up_swa", "w_up_fox", "w_out",
        "g_post"]


def constants():
    def bf16_bits(a):
        return (np.ascontiguousarray(a, np.float32).view(np.uint32) >> 16).astype(np.uint16)

    slopes = 2.0 ** -np.arange(1, HEADS + 1)
    ident = np.eye(P, dtype=np.float32)
    a, c = np.arange(P)[:, None], np.arange(P)[None, :]
    causal = np.where(c <= a, 0.0, MASK)
    meta = N_META + a - np.arange(N_META)[None, :]
    back = a - (np.arange(CHUNK)[None, :] - CHUNK)
    dist = np.concatenate([meta, back, np.abs(a - c)], axis=1)
    ok = np.concatenate([np.ones((P, N_META), bool), np.broadcast_to(a < CHUNK, (P, CHUNK)),
                         (c // CHUNK) <= (a // CHUNK)], axis=1)
    alibi = np.where(ok[:, None, :], -slopes[None, :, None] * dist[:, None, :], MASK)
    const = bf16_bits(np.concatenate([ident, causal, alibi.reshape(P, -1)], axis=1))
    first = np.where(np.arange(A_ROWS) < N_META, 0.0, MASK)
    far = -slopes[:, None] * P * np.arange(NQ)[None, :]
    rows = bf16_bits(np.concatenate([np.ones(P), first, far.reshape(-1)])[None, :])
    return {"ident": ident, "const": const, "rows": rows}


def kernel(**inputs):
    import concourse.bacc as _bacc
    from concourse.bass_utils import run_bass_kernel_spmd as _run

    nc = _bacc.Bacc("TRN2", target_bir_lowering=False, num_devices=1)
    arrays, args = {}, []
    data = {n: np.ascontiguousarray(inputs[n]) for n in _INS}
    data.update(constants())
    for name, a in data.items():
        arrays[f"in_{name}_dram"] = a
        args.append(nc.dram_tensor(f"in_{name}_dram", a.shape, mybir.dt.from_np(a.dtype), kind="ExternalInput").ap())
    args.append(nc.dram_tensor("out_dram", (1, SEQ, D_MODEL), F32, kind="ExternalOutput").ap())
    build(nc, *args)
    return _run(nc, [arrays], core_ids=[0]).results[0]["out_dram"]
```
